# Optimizing a Trainium2 kernel written in Bass

```python
import jax, jax.numpy as jnp
from jax import lax
import numpy as np

D_MODEL = 2048
BATCH = 1
SEQ = 128
DEPTH = 2
DEC_BATCH = 1
DEC_SEQ = 512
PAST_LEN = 128

GRID_W = 64
N_HEADS = 16
N_KV_HEADS = 4
HEAD_DIM = 128
GROUP = N_HEADS // N_KV_HEADS
BRANCH = N_HEADS * HEAD_DIM
KV_W = N_KV_HEADS * HEAD_DIM
PROJ_W = 2 * BRANCH + 2 * KV_W
N_MIXERS = 2
N_WINDOW_LAYERS = (DEPTH + 1) // 2
WINDOW = 128
Q_BLOCK = 128
ROPE_THETA = 10000.0
EPS = 1e-6
NEG_INF = -1e30

kernel_name = "hybrid_dit_prefix_window_axial_gqa_step"

def rmsnorm(x, g):
    xf = x.astype(jnp.float32)
    y = xf * lax.rsqrt(jnp.mean(xf * xf, axis=-1, keepdims=True) + EPS)
    return (y * g.astype(jnp.float32)).astype(x.dtype)

def axial_rope_tables(n_tokens):
    rows = n_tokens // GRID_W
    row = jnp.repeat(jnp.arange(rows), GRID_W).astype(jnp.float32)
    col = jnp.tile(jnp.arange(GRID_W), rows).astype(jnp.float32)
    n_freq = HEAD_DIM // 4
    inv = ROPE_THETA ** (-jnp.arange(n_freq, dtype=jnp.float32) / n_freq)
    ang = jnp.stack([row[:, None] * inv, col[:, None] * inv], axis=1)
    return jnp.cos(ang), jnp.sin(ang)

def apply_axial_rope(x, cos, sin):
    b, t, h, d = x.shape
    xf = x.astype(jnp.float32).reshape(b, t, h, 2, 2, d // 4)
    x1, x2 = xf[..., 0, :], xf[..., 1, :]
    cs, sn = cos[:, None], sin[:, None]
    out = jnp.stack([x1 * cs - x2 * sn, x2 * cs + x1 * sn], axis=-2)
    return out.reshape(b, t, h, d).astype(x.dtype)

def attend(q, k, v, mask, sink):
    s = jnp.einsum('bqhgd,bkhd->bhgqk', q, k, preferred_element_type=jnp.float32) * (HEAD_DIM ** -0.5)
    if mask is not None:
        s = jnp.where(mask, s, NEG_INF)
    if sink is not None:
        sk = jnp.broadcast_to(sink.astype(jnp.float32)[None, :, :, None, None], s.shape[:-1] + (1,))
        p = jax.nn.softmax(jnp.concatenate([s, sk], axis=-1), axis=-1)[..., :-1]
    else:
        p = jax.nn.softmax(s, axis=-1)
    return jnp.einsum('bhgqk,bkhd->bqhgd', p.astype(v.dtype), v)

def to_blocks(q):
    b, t = q.shape[:2]
    return q.reshape(b, t // Q_BLOCK, Q_BLOCK, *q.shape[2:]).swapaxes(0, 1)

def from_blocks(o):
    nb, b = o.shape[:2]
    return o.swapaxes(0, 1).reshape(b, nb * Q_BLOCK, BRANCH)

def dense_attention(q, k, v, sink):
    o = lax.map(lambda qb: attend(qb, k, v, None, sink), to_blocks(q))
    return from_blocks(o)

def window_attention(q, k, v, k_ctx, v_ctx, sink):
    t = q.shape[1]
    nb = t // Q_BLOCK
    pad = ((0, 0), (WINDOW, WINDOW), (0, 0), (0, 0))
    k_pad, v_pad = jnp.pad(k, pad), jnp.pad(v, pad)
    span = Q_BLOCK + 2 * WINDOW
    i = jnp.arange(Q_BLOCK)[:, None]
    j = jnp.arange(span)[None, :]
    band = (j - i >= 0) & (j - i <= 2 * WINDOW)
    ctx_ok = jnp.ones((Q_BLOCK, k_ctx.shape[1]), dtype=bool)

    def block(args):
        qb, blk = args
        start = blk * Q_BLOCK
        kb = lax.dynamic_slice_in_dim(k_pad, start, span, axis=1)
        vb = lax.dynamic_slice_in_dim(v_pad, start, span, axis=1)
        pos = start - WINDOW + j
        mask = jnp.concatenate([band & (pos >= 0) & (pos < t), ctx_ok], axis=1)
        return attend(qb, jnp.concatenate([kb, k_ctx], axis=1),
                      jnp.concatenate([vb, v_ctx], axis=1), mask, sink)

    o = lax.map(block, (to_blocks(q), jnp.arange(nb)))
    return from_blocks(o)

def branch_in(x, mod, norm_g, w_in, q_g, k_g):
    shift, scale, gate = jnp.split(mod, 3, axis=-1)
    h = rmsnorm(x, norm_g) * (1 + scale[:, None]) + shift[:, None]
    proj = h @ w_in
    q, z, k, v = jnp.split(proj, [BRANCH, 2 * BRANCH, 2 * BRANCH + KV_W], axis=-1)
    b, t = x.shape[:2]
    q = rmsnorm(q.reshape(b, t, N_HEADS, HEAD_DIM), q_g)
    k = rmsnorm(k.reshape(b, t, N_KV_HEADS, HEAD_DIM), k_g)
    v = v.reshape(b, t, N_KV_HEADS, HEAD_DIM)
    return q, z, k, v, gate

def group_q(q):
    b, t = q.shape[:2]
    return q.reshape(b, t, N_KV_HEADS, GROUP, HEAD_DIM)

def branch_out(x, attn, z, gate, w_out):
    y = (attn * jax.nn.silu(z)) @ w_out
    return x + gate[:, None] * y

def setup_inputs(seed: int = 0) -> dict:
    key = jax.random.key(seed)
    ks = jax.random.split(key, 14)
    f32 = jnp.float32
    cache_shape = (DEC_BATCH, DEPTH, PAST_LEN, N_KV_HEADS, HEAD_DIM)
    return {
        "x_prompt": jax.random.normal(ks[0], (BATCH, SEQ, D_MODEL), f32),
        "x_sample": jax.random.normal(ks[1], (DEC_BATCH, DEC_SEQ, D_MODEL), f32),
        "c": jax.random.normal(ks[2], (DEC_BATCH, D_MODEL), f32),
        "cache_k": jax.random.normal(ks[3], cache_shape, f32),
        "cache_v": jax.random.normal(ks[4], cache_shape, f32),
        "c_ctx": jax.random.normal(ks[5], (D_MODEL,), f32),
        "norm_g": 1.0 + 0.02 * jax.random.normal(ks[6], (DEPTH, D_MODEL), f32),
        "w_mod": 0.5 * D_MODEL ** -0.5 * jax.random.normal(ks[7], (DEPTH, D_MODEL, 3 * D_MODEL), f32),
        "b_mod": 0.02 * jax.random.normal(ks[8], (DEPTH, 3 * D_MODEL), f32),
        "w_in": D_MODEL ** -0.5 * jax.random.normal(ks[9], (DEPTH, D_MODEL, PROJ_W), f32),
        "q_norm_g": 1.0 + 0.02 * jax.random.normal(ks[10], (DEPTH, HEAD_DIM), f32),
        "k_norm_g": 1.0 + 0.02 * jax.random.normal(ks[11], (DEPTH, HEAD_DIM), f32),
        "sinks": jax.random.normal(ks[12], (N_WINDOW_LAYERS, N_HEADS), f32),
        "w_out": BRANCH ** -0.5 * jax.random.normal(ks[13], (DEPTH, BRANCH, D_MODEL), f32),
    }

def reference(x_prompt, x_sample, c, cache_k, cache_v, c_ctx, norm_g, w_mod, b_mod, w_in,
              q_norm_g, k_norm_g, sinks, w_out):
    rope = axial_rope_tables(x_sample.shape[1])
    xp, xs = x_prompt, x_sample
    new_k, new_v = [], []
    for l in range(DEPTH):
        use_window = (l % N_MIXERS) == 0
        sink = sinks[l // N_MIXERS].reshape(N_KV_HEADS, GROUP) if use_window else None

        mod_c = (jax.nn.silu(c_ctx) @ w_mod[l] + b_mod[l])[None]
        q, z, k, v, gate = branch_in(xp, mod_c, norm_g[l], w_in[l], q_norm_g[l], k_norm_g[l])
        attn = dense_attention(group_q(q), k, v, sink)
        xp = branch_out(xp, attn, z, gate, w_out[l])
        new_k.append(k)
        new_v.append(v)

        mod_s = jax.nn.silu(c) @ w_mod[l] + b_mod[l]
        q, z, k, v, gate = branch_in(xs, mod_s, norm_g[l], w_in[l], q_norm_g[l], k_norm_g[l])
        q = group_q(apply_axial_rope(q, *rope))
        k = apply_axial_rope(k, *rope)
        k_ctx, v_ctx = cache_k[:, l], cache_v[:, l]
        if use_window:
            attn = window_attention(q, k, v, k_ctx, v_ctx, sink)
        else:
            attn = dense_attention(q, jnp.concatenate([k, k_ctx], axis=1),
                                   jnp.concatenate([v, v_ctx], axis=1), None)
        xs = branch_out(xs, attn, z, gate, w_out[l])

    new_cache_k = jnp.stack(new_k, axis=1)
    new_cache_v = jnp.stack(new_v, axis=1)
    return (xp, xs, new_cache_k, new_cache_v)


_drawn_inputs = setup_inputs


def setup_inputs(seed=0):
    import zlib

    import numpy as np

    out = dict(_drawn_inputs(seed))
    spreads = {}
    factors = {'cache_k': 5.351,
     'cache_v': 4.281,
     'norm_g': 2.9,
     'q_norm_g': 8.0,
     'k_norm_g': 2.82,
     'sinks': 8.0}
    for name, (base, spread) in spreads.items():
        noise = np.random.default_rng([zlib.crc32(name.encode()), seed]).standard_normal(out[name].shape)
        drawn = base * np.exp(spread * noise) if base else spread * noise
        out[name] = __import__('jax').numpy.asarray(drawn.astype(out[name].dtype))
    for name, factor in factors.items():
        out[name] = (out[name] * factor).astype(out[name].dtype)
    return out
```

```python
import numpy as np
import concourse.bass as bass
from concourse import mybir
from contextlib import ExitStack

P = 128
D = 2048
KT = D // P
TOK = 4
TT = TOK + 1
HEADS, KVH, GROUP = 16, 4, 4
NC = 512
PROJ = 5120
PAIRS = KT // 2
LAYERS = 2
N_CHUNKS = 14
FIRST_Z, FIRST_O = 6, 10
MODB = 1024
MODS = 3 * D // MODB
EPS = 1e-6
SCALE = P ** -0.5
NEG = -1e30
CTX, REQ = TOK * P, TT * P
KCOLS = 6 * P
CREDIT = 5
N_TR = 46


def build(nc, x_prompt, x_sample, c, cache_k, cache_v, c_ctx, norm_g, w_mod, b_mod, w_in, q_norm_g,
          k_norm_g, sinks, w_out, rope_cos, rope_sin, y_prompt, y_sample, new_k, new_v):
    f32, f32r, bf16 = mybir.dt.float32, mybir.dt.float32r, mybir.dt.bfloat16
    ALU, ACT, AX = mybir.AluOpType, mybir.ActivationFunctionType, mybir.AxisListType.X
    ds = bass.ds
    ctx = ExitStack()
    with ctx:
        def sb(name, shape, dt=f32):
            return ctx.enter_context(nc.sbuf_tensor(name, shape, dt))

        def sem(name):
            return ctx.enter_context(nc.semaphore(name))

        mod_rows = nc.dram_tensor("mod_rows", [2, LAYERS * 3 * D], f32, kind="Internal").ap()
        z_spill = nc.dram_tensor("z_spill", [KVH, TT, P, NC], f32, kind="Internal").ap()
        x_spill = nc.dram_tensor("x_spill", [TT, P, D], f32, kind="Internal").ap()

        def phase(*tensors):
            with ExitStack() as shared:
                return [shared.enter_context(nc.sbuf_tensor(*t)) for t in tensors]

        region = ("region", [P, 2 * KT * TT * P], f32)
        hT_hi, hT_lo = phase(*[(f"hT_{n}", [P, KT, TT * P], f32r) for n in ("hi", "lo")])
        first_ring, = phase(("first_ring", [P, PAIRS, 2, MODB], f32))
        a = phase(("probs0", [P, 4, 5 * P], f32), ("probs1", [P, 4, 5 * P], f32), ("probs2", [P, 4, P], f32),
                  ("probsT0", [P, 5, NC], f32), ("probsT1", [P, 5, NC], f32), ("probsT2", [P, 1, NC], f32),
                  ("z_in", [P, TT, NC], f32), ("v_g", [P, 6, P], f32),
                  ("k_hi", [P, KCOLS], f32r), ("k_lo", [P, KCOLS], f32r),
                  *[(f"q_{n}{b}", [P, NC], f32r) for n in ("hi", "lo") for b in range(3)])
        probs, probsT, (z_in, v_g, k_hi, k_lo), q_hi, q_lo = a[0:3], a[3:6], a[6:10], a[10:13], a[13:16]
        ctx.enter_context(nc.sbuf_tensor(*region))

        qT_x = sb("qT_x", [P, KVH * TT * NC])
        qT = qT_x[:, :].rearrange("p (g t n) -> p g t n", g=KVH, t=TT)
        x_tok = qT_x[:, :].rearrange("p (t n) -> p t n", t=TT)
        kT = sb("kT", [P, KVH, KCOLS])
        v_tok = sb("v_tok", [P, 6, NC])
        w_raw = sb("w_raw", [P, 2, 2, NC])
        w_hi = sb("w_hi", [P, 2, 2, NC], f32r)
        w_lo = sb("w_lo", [P, 2, 2, NC], f32r)
        mod_ring = sb("mod_ring", [P, 2 * 2048])
        mod_w = mod_ring[:, :].rearrange("p (s k n) -> p s k n", s=2, k=2)
        x_old = mod_ring[:, 0:TT * NC].rearrange("p (t n) -> p t n", t=TT)
        gate = mod_ring[:, 2560:3584].rearrange("p (r n) -> p r n", r=2)
        gate_b = mod_ring[:, 3584:4096]
        stage = sb("stage", [P, TT, NC])
        h32 = stage[:, :, :].rearrange("p t n -> p (t n)")[:, 0:2 * TT * P].rearrange("p (s n) -> p s n", s=2)
        t1, t2 = sb("t1", [P, NC]), sb("t2", [P, NC])
        rope_c, rope_s = sb("rope_c", [P, TOK, P]), sb("rope_s", [P, TOK, P])
        gain = sb("gain", [P, P])
        mod_ev = sb("mod_ev", [P, MODB // 4])
        ident = sb("ident", [P, P])
        ident_b, mask_prev, mask_next = (sb(n, [P, P], bf16) for n in ("ident_b", "mask_prev", "mask_next"))
        consts = sb("consts", [P, P])
        rows = sb("rows", [P, P])
        cond = sb("cond", [P, KT, 2])
        mulA, addB = sb("mulA", [P, KT, 2]), sb("addB", [P, KT, 2])
        junk, eps = sb("junk", [P, P]), sb("eps", [P, 1])
        ss_x, ss_h = sb("ss_x", [P, TT, 4]), sb("ss_h", [P, TT, 4])
        rms_x, rms_h = sb("rms_x", [P, TT]), sb("rms_h", [P, TT, 4])
        sum_x, r_x, r_h = sb("sum_x", [P, TT]), sb("r_x", [P, TT]), sb("r_h", [P, 4])
        sink, neg_sink = sb("sink", [P, HEADS]), sb("neg_sink", [P, HEADS])
        mx, mxc, nmax, den, denx, sinkd, rden = (sb(n, [P, 4]) for n in
                                                 ("mx", "mxc", "nmax", "den", "denx", "sinkd", "rden"))
        bank = [ctx.enter_context(nc.psum_tensor(f"bank{i}", [P, 512], f32)) for i in range(8)]
        MODBANK = 5

        s_rows, s_x, s_sink = sem("s_rows"), sem("s_x"), sem("s_sink")
        s_first = [sem(f"s_first{i}") for i in range(8)]
        s_w = [sem(f"s_w{i}") for i in range(2)]
        s_mw = [sem(f"s_mw{i}") for i in range(2)]
        s_modout, s_modin, s_tab, s_ck, s_cv = (sem(n) for n in ("s_modout", "s_modin", "s_tab", "s_ck", "s_cv"))
        s_newk, s_newv, s_y = sem("s_newk"), sem("s_newv"), sem("s_y")
        s_zout, s_zin = [sem(f"s_zout{i}") for i in range(2)], [sem(f"s_zin{i}") for i in range(TT)]
        s_old = sem("s_old")
        const_made, consts_T, consts_ready, cond_ready = (sem(n) for n in
                                                          ("const_made", "consts_T", "consts_ready", "cond_ready"))
        first_used, mod_used, mod_evac = sem("first_used"), sem("mod_used"), sem("mod_evac")
        modT_done, ab_ready = sem("modT_done"), sem("ab_ready")
        xsq_done, x_normed, x_new, xsq_l1 = (sem(n) for n in ("xsq_done", "x_normed", "x_new", "xsq_l1"))
        x_summed, x_rooted = sem("x_summed"), sem("x_rooted")
        h_tr, h_ev, h_ready = sem("h_tr"), sem("h_ev"), sem("h_ready")
        whi_ready, wlo_ready, mm_done, acc_done, acc_free = (sem(n) for n in
                                                             ("whi_ready", "wlo_ready", "mm_done", "acc_done", "acc_free"))
        ss_ready, roped, tr_done, tr_free, tab_ready = (sem(n) for n in
                                                        ("ss_ready", "roped", "tr_done", "tr_free", "tab_ready"))
        gate_ready = sem("gate_ready")
        sc_done, nm_ready, exp_done, pn_ready = (sem(n) for n in ("sc_done", "nm_ready", "exp_done", "pn_ready"))
        scx_done, pt_done, pt_act, pt_dve = (sem(n) for n in ("scx_done", "pt_done", "pt_act", "pt_dve"))
        o_done, gated, q_split, kv_main, kv_req = (sem(n) for n in ("o_done", "gated", "q_split", "kv_main", "kv_req"))
        dve_chain, act_chain, pool_chain = sem("dve_chain"), sem("act_chain"), sem("pool_chain")

        class Chain:

            def __init__(self, s):
                self.s, self.base, self.k, self.i, self.per = s, 0, 0, 0, 0

            def link(self, eng, ins):
                ins.then_inc(self.s, 1)
                self.k += 1
                eng.wait_ge(self.s, self.i * self.per + (self.base + self.k) if self.per else self.base + self.k)

            def enter(self, i, first, per):
                self.base += self.k - first * per
                self.k, self.i, self.per = 0, i, per

            def leave(self, end):
                assert self.k == self.per, (self.k, self.per)
                self.base += end * self.per
                self.k, self.per = 0, 0

        def w_col(ch):
            return {0: 4096, 1: 4608}.get(ch) if isinstance(ch, int) and ch < 2 else (ch - 2) * NC

        def key_parts(L, u):
            if u == TOK:
                return [(REQ, P)]
            if L == 1:
                return [(0, NC)]
            lo, hi = max(0, u - 1) * P, min(TOK, u + 2) * P
            return [(lo, CTX + P - lo)] if hi == CTX else [(lo, hi - lo), (CTX, P)]

        def key_tiles(L, u):
            if u == TOK:
                return [5]
            if L == 1:
                return [0, 1, 2, 3, 4]
            return list(range(max(0, u - 1), min(TOK, u + 2))) + [4]

        n_kt = [[len(key_tiles(L, u)) for u in range(TT)] for L in range(LAYERS)]
        n_even = [[(n + 1) // 2 for n in row] for row in n_kt]
        n_odd = [[n // 2 for n in row] for row in n_kt]

        def before(table, L, g, u):
            return sum(4 * sum(table[l]) for l in range(L)) + g * sum(table[L]) + sum(table[L][:u])

        def unit(L, g, u):
            return g * TT + (20 * L + u)

        def same_buffer(L, g, u):
            return unit(L, g, u) - (TT if u == TOK else 2 if u >= 2 else 3)

        Z_STORES = (3, 2)

        def buf(u):
            return 2 if u == TOK else u % 2

        def tr_number(L, X, t):
            return X * TT + (N_TR * L + t + (1 if not (isinstance(X, int) and X == 0) else 0))

        H0 = [0, 2 * KT]

        block = ctx.enter_context(nc.Block())

        @block.sync
        def _(sp):
            def mod_src(col, k0, L):
                return w_mod[L, k0 * P:(k0 + 2) * P, ds(col, MODB)].rearrange("(k p) n -> p k n", p=P)

            def first_load(b, s, wait):
                if wait:
                    sp.wait_ge(first_used, b * PAIRS + (s + 1 - PAIRS))
                sp.dma_start(first_ring[:, s], mod_src(b * MODB, 2 * s, 0)).then_inc(s_first[s], 16)

            for s in range(PAIRS):
                first_load(0, s, False)
            with sp.Fori(1, 4) as b:
                for s in range(PAIRS):
                    first_load(b, s, True)

            def chunk_loads(L, ch, src, n0, mod=None):
                for p in range(PAIRS):
                    if not (isinstance(ch, int) and L == 0 and ch == 0 and p < 2):
                        sp.wait_ge(wlo_ready, (ch + 14 * L) * PAIRS + (p - 1))
                    sp.dma_start(w_raw[:, p % 2], src[L, 2 * p * P:(2 * p + 2) * P, ds(n0, NC)]
                                 .rearrange("(k p) n -> p k n", p=P)).then_inc(s_w[p % 2], 16)
                    if mod is not None:
                        number, ml, mb = mod
                        if not (isinstance(number, int) and number == 0 and p < 2):
                            sp.wait_ge(mod_used, number * PAIRS + (p - 1))
                        sp.dma_start(mod_w[:, p % 2], mod_src(mb * MODB, 2 * p, ml)).then_inc(s_mw[p % 2], 16)

            for L in range(LAYERS):
                for ch in (0, 1):
                    if L == 1 and ch == 0:
                        sp.wait_ge(x_new, TT * 4)
                    chunk_loads(L, ch, w_in, w_col(ch), (6 * L + ch, L, 4 + ch))
                chunk_loads(L, 2, w_in, 0, (2, 1, 0) if L == 0 else None)
                with sp.Fori(1, 4) as i:
                    chunk_loads(L, i + 2, w_in, i * NC, (i + 2, 1, i) if L == 0 else None)
                chunk_loads(L, FIRST_Z, w_in, D, None)
                with sp.Fori(1, 4) as i:
                    chunk_loads(L, i + FIRST_Z, w_in, i * NC + D, None)
                chunk_loads(L, FIRST_O, w_out, 0, None)
                with sp.Fori(1, 4) as i:
                    chunk_loads(L, i + FIRST_O, w_out, i * NC, None)

        @block.gpsimd
        def _(pool):
            chain = Chain(pool_chain)
            g = nc.gpsimd
            g.memset(eps[:], EPS)
            for t in (ident, ident_b, mask_prev, mask_next):
                chain.link(pool, g.memset(t[:], 0.0))
            for t in (ident, ident_b):
                chain.link(pool, g.affine_select(out=t[:], in_=t[:], compare_op=ALU.not_equal, fill=1.0, base=0,
                                                 pattern=[[-1, P]], channel_multiplier=1))
            chain.link(pool, g.affine_select(out=mask_prev[:], in_=mask_prev[:], compare_op=ALU.is_ge, fill=NEG,
                                             base=0, pattern=[[1, P]], channel_multiplier=-1))
            g.affine_select(out=mask_next[:], in_=mask_next[:], compare_op=ALU.is_ge, fill=NEG, base=0,
                            pattern=[[-1, P]], channel_multiplier=1).then_inc(const_made, 1)
            pool.dma_start(rows[0:16, :], c.rearrange("a (j p) -> (a j) p", p=P)).then_inc(s_rows, 16)
            pool.dma_start(rows[16:32, :], c_ctx.rearrange("(j p) -> j p", p=P)).then_inc(s_rows, 16)
            pool.dma_start(rows[32:64, :], norm_g.rearrange("l (j p) -> (l j) p", p=P)).then_inc(s_rows, 16)
            for L in range(LAYERS):
                pool.dma_start(rows[64 + 32 * L:96 + 32 * L, :],
                               b_mod[L, 0:2 * D].rearrange("(j p) -> j p", p=P)).then_inc(s_rows, 16)
            pool.dma_start(sink[:, :], sinks[0:1, :].to_broadcast([P, HEADS])).then_inc(s_sink, 16)

            def mod_store(Q):
                pool.wait_ge(mod_evac, Q + 1)
                for r in range(2):
                    pool.dma_start(mod_rows[r:r + 1, ds(Q * MODB, MODB)].rearrange("r (j n) -> (r j) n", j=4),
                                   mod_ev[r:r + 97:32, :]).then_inc(s_modout, 16)

            def mod_rows_in(L):
                if L == 0:
                    pool.wait_ge(consts_T, 1)
                pool.wait_ge(s_modout, 32 * (MODS * L + 4))
                for r in range(2):
                    pool.dma_start(rows[32 * r:32 * r + 32, :],
                                   mod_rows[r:r + 1, L * 3 * D:L * 3 * D + 2 * D].rearrange("r (j p) -> (r j) p", p=P)
                                   ).then_inc(s_modin, 16)

            def table_loads(n, norm):
                if n > 0:
                    pool.wait_ge(roped, 5 if n == 1 else 25 if n == 2 else 30)
                pool.dma_start(rope_c[:, :, :], rope_cos.rearrange("(t p) d -> p t d", p=P)).then_inc(s_tab, 16)
                pool.dma_start(rope_s[:, :, :], rope_sin.rearrange("(t p) d -> p t d", p=P)).then_inc(s_tab, 16)
                pool.dma_start(gain[:, :], norm.to_broadcast([P, P])).then_inc(s_tab, 16)

            def z_stores(L, X):
                for t in range(TT):
                    pool.wait_ge(tr_free, tr_number(L, X, t) + 1)
                    pool.dma_start(z_spill[ds(X - 5, 1), t].rearrange("g p n -> (g p) n"),
                                   (t1, t2)[t % 2][:, :]).then_inc(s_zout[t % 2], 16)

            table_loads(0, k_norm_g[0:1, :])
            for Q in range(4):
                mod_store(Q)
            mod_rows_in(0)

            for L in range(LAYERS):
                mod_store(4 if L == 0 else 10)
                pool.wait_ge(roped, 25 * L + TT)
                pool.dma_start(new_k[0, L].rearrange("p h d -> p (h d)"), stage[:, TOK, :]).then_inc(s_newk, 16)
                pool.dma_start(v_tok[:, 4, :], cache_v[0, L].rearrange("p h d -> p (h d)")).then_inc(s_cv, 16)
                mod_store(5 if L == 0 else 11)
                pool.wait_ge(tr_done, tr_number(L, 0, 4) + 1)
                pool.dma_start(stage[:, 0, :], cache_k[0, L].rearrange("p h d -> p (h d)")).then_inc(s_ck, 16)
                table_loads(2 * L + 1, q_norm_g[L:L + 1, :])
                pool.wait_ge(acc_free, (14 * L + 2) * TT)
                pool.dma_start(new_v[0, L].rearrange("p h d -> p (h d)"), v_tok[:, 5, :]).then_inc(s_newv, 16)
                if L == 0:
                    mod_store(6)
                    with pool.Fori(1, 4) as i:
                        mod_store(i + 6)
                    table_loads(2, k_norm_g[1:2, :])
                for X in (5, 6, 7):
                    z_stores(L, X)

                def k_split(gg, first, n, prev, done):
                    pool.wait_ge(sc_done, prev * 4 + (4 * CREDIT + 4))
                    src = kT[:, ds(gg, 1), first:first + n].rearrange("p g k -> p (g k)")
                    g.tensor_copy(k_hi[:, first:first + n], src)
                    pool.drain()
                    g.tensor_tensor(k_lo[:, first:first + n], src, k_hi[:, first:first + n].bitcast(f32),
                                    ALU.subtract).then_inc(done, 1)

                def v_copy(gg, first, n, prev, done):
                    pool.wait_ge(o_done, prev + (CREDIT + 1))
                    g.tensor_copy(v_g[:, first // P:(first + n) // P, :],
                                  v_tok[:, first // P:(first + n) // P, ds(gg * P, P)]).then_inc(done, 1)

                def q_split_unit(gg, u):
                    U, prev = unit(L, gg, u), same_buffer(L, gg, u)
                    pool.wait_ge(sc_done, prev * 4 + (4 * CREDIT + 4))
                    src = qT[:, ds(gg, 1), u, :].rearrange("p g n -> p (g n)")
                    g.tensor_copy(q_hi[buf(u)][:, :], src)
                    pool.drain()
                    g.tensor_tensor(q_lo[buf(u)][:, :], src, q_hi[buf(u)][:, :].bitcast(f32), ALU.subtract).then_inc(q_split, 1)

                def z_load(gg, u):
                    pool.wait_ge(gated, unit(L, gg, u) + (CREDIT - TT + 1))
                    pool.dma_start(z_in[:, u, :], z_spill[ds(gg, 1), u].rearrange("g p n -> (g p) n")
                                   ).then_inc(s_zin[u], 16)

                pool.wait_ge(acc_done, (14 * L + FIRST_O) * TT)
                pool.wait_ge(tr_free, tr_number(L, 4, 4) + 1)
                pool.wait_ge(s_cv, 16 * (L + 1))
                k_split(0, 0, 5 * P, unit(L, 0, 0) - 2, kv_main)
                q_split_unit(0, 0)
                v_copy(0, 0, 5 * P, unit(L, 0, 0) - 2, kv_main)
                z_stores(L, 8)
                for i in range(2):
                    pool.wait_ge(s_zout[i], 64 * Z_STORES[i] * (L + 1))

                def pool_group(gg, last):
                    for u in range(TT):
                        z_load(gg, u)
                        if u < TOK:
                            q_split_unit(gg, u + 1)
                        elif not last:
                            k_split(gg + 1, 0, 5 * P, unit(L, gg, 3), kv_main)
                            q_split_unit(gg + 1, 0)
                            v_copy(gg + 1, 0, 5 * P, unit(L, gg, 3), kv_main)
                        if u == 0:
                            k_split(gg, REQ, P, unit(L, gg, 0) - 1, kv_req)
                            v_copy(gg, REQ, P, unit(L, gg, 0) - 1, kv_req)

                with pool.Fori(0, 3) as gg:
                    pool_group(gg, False)
                pool_group(3, True)

                def out_loads(n):
                    if isinstance(n, int) and n == 0:
                        pool.wait_ge(mod_used, PAIRS * (6 if L == 0 else 8))
                        pool.wait_ge(s_modout, 32 * (10 if L == 0 else 12))
                        if L == 1:
                            pool.wait_ge(s_y, 16 * TT * 4)
                    else:
                        pool.wait_ge(x_new, n * TT + 20 * L)
                    for t in range(TT):
                        if L == 1:
                            src = x_spill[t, :, ds(n * NC, NC)]
                        elif t < TOK:
                            src = x_sample[0, t * P:(t + 1) * P, ds(n * NC, NC)]
                        else:
                            src = x_prompt[0, :, ds(n * NC, NC)]
                        pool.dma_start(x_old[:, t, :], src).then_inc(s_old, 16)
                    col = n * NC + (3 * D * L + 2 * D)
                    for r in range(2):
                        pool.dma_start(gate[:, r, :], mod_rows[r:r + 1, ds(col, NC)].to_broadcast([P, NC])
                                       ).then_inc(s_old, 16)
                    pool.dma_start(gate_b, b_mod[L:L + 1, ds(n * NC + 2 * D, NC)].to_broadcast([P, NC])
                                   ).then_inc(s_old, 16)

                def out_stores(n):
                    for t in range(TT):
                        pool.wait_ge(x_new, n * TT + (20 * L + t + 1))
                        if L == 0:
                            dst = x_spill[t, :, ds(n * NC, NC)]
                        elif t < TOK:
                            dst = y_sample[0, t * P:(t + 1) * P, ds(n * NC, NC)]
                        else:
                            dst = y_prompt[0, :, ds(n * NC, NC)]
                        pool.dma_start(dst, x_tok[:, t, ds(n * NC, NC)]).then_inc(s_y, 16)

                if L == 0:
                    mod_rows_in(1)
                out_loads(0)
                out_stores(0)
                with pool.Fori(1, 4) as n:
                    out_loads(n)
                    out_stores(n)

            pool.wait_ge(s_newk, 16 * LAYERS)
            pool.wait_ge(s_newv, 16 * LAYERS)
            pool.wait_ge(s_y, 16 * TT * 4 * LAYERS)
            pool.wait_ge(s_modout, 32 * 12)
            for i in range(2):
                pool.wait_ge(s_zout[i], 64 * Z_STORES[i] * LAYERS)

        @block.scalar
        def _(act):
            chain = Chain(act_chain)
            s = nc.scalar
            for t in range(TT):
                src = x_sample[0, t * P:(t + 1) * P, :] if t < TOK else x_prompt[0]
                act.dma_start(x_tok[:, t, :], src).then_inc(s_x, 16)
            act.wait_ge(consts_ready, 1)
            s.activation(cond[:, :, :].rearrange("p k r -> p r k"), consts[:, 0:32].rearrange("p (r k) -> p r k", r=2),
                         ACT.Silu).then_inc(cond_ready, 1)

            def x_square(t, n):
                s.activation(stage[:, t, :], x_tok[:, t, n * NC:(n + 1) * NC] if isinstance(n, int)
                             else x_tok[:, t, ds(n * NC, NC)], ACT.Square,
                             accum_out=ss_x[:, t, ds(n, 1)] if not isinstance(n, int) else ss_x[:, t, n:n + 1])

            act.wait_ge(s_x, 16 * TT)
            for n in range(4):
                for t in range(TT):
                    ins = s.activation(stage[:, t, :], x_tok[:, t, n * NC:(n + 1) * NC], ACT.Square,
                                       accum_out=ss_x[:, t, n:n + 1])
                    if t == TT - 1 and n < 3:
                        chain.link(act, ins)
                    elif t == TT - 1:
                        ins.then_inc(xsq_done, 1)

            def mod_evacuate(used, count, Q):
                act.wait_ge(used, count)
                if not (isinstance(Q, int) and Q == 0):
                    act.wait_ge(s_modout, Q * 32)
                for j in range(4):
                    ins = s.copy(mod_ev[32 * j:32 * j + 2, :], bank[MODBANK][32 * j:32 * j + 2, 0:256])
                ins.then_inc(mod_evac, 1)

            mod_evacuate(first_used, PAIRS, 0)
            with act.Fori(1, 4) as b:
                mod_evacuate(first_used, b * PAIRS + PAIRS, b)

            def split_hi(L, ch, p):
                C = ch + 14 * L
                act.wait_ge(s_w[p % 2], C * 64 + 16 * (p // 2 + 1))
                start = isinstance(ch, int) and L == 0 and ch == 0
                if p == 0 and not start:
                    act.wait_ge(mm_done, C * 7)
                elif p == 1 and not start:
                    act.wait_ge(acc_done, C * TT)
                elif p >= 2:
                    act.wait_ge(mm_done, C * 7 + (p - 1))
                s.copy(w_hi[:, p % 2], w_raw[:, p % 2]).then_inc(whi_ready, 1)

            def evacuate(L, ch, kind, X):
                C = ch + 14 * L
                for t in range(TT):
                    act.wait_ge(acc_done, C * TT + (t - 4))
                    if kind == "v":
                        s.copy(v_tok[:, t if t < TOK else 5, :], bank[t][:, :]).then_inc(acc_free, 1)
                        continue
                    if kind == "k":
                        act.wait_ge(h_ready, H0[L] + KT)
                    else:
                        act.wait_ge(tr_done, X * TT + (N_TR * L + t - TT + 2))
                    s.activation(stage[:, t, :], bank[t][:, :], ACT.Silu if kind == "z" else ACT.Copy
                                 ).then_inc(acc_free, 1)

            def head_squares(L, X):
                R = X * TT + 25 * L
                if not (isinstance(X, int) and X == 0 and L == 0):
                    act.wait_ge(roped, R)
                act.wait_ge(acc_free, (14 * L + 1 + X + (0 if isinstance(X, int) and X == 0 else 1)) * TT)
                for t in range(TT):
                    for h in range(4):
                        chain.link(act, s.activation(junk[:, :], stage[:, t, h * P:(h + 1) * P], ACT.Square,
                                                     accum_out=ss_h[:, t, h:h + 1]))
                    s.activation(rms_h[:, t, :], ss_h[:, t, :], ACT.Sqrt, bias=eps[:, :], scale=1.0 / P
                                 ).then_inc(ss_ready, 1)

            def evac_transposed(L, kind, X, t):
                n = tr_number(L, X, t)
                act.wait_ge(tr_done, n + 1)
                src = bank[6 + t % 2]
                if kind == "k":
                    col = t * P if t < TOK else REQ
                    dst, src = kT[:, :, col:col + P], src[:, :].rearrange("p (g n) -> p g n", g=4)
                elif kind == "q":
                    dst, src = qT[:, ds(X - 1, 1), t, :].rearrange("p g n -> p (g n)"), src[:, :]
                else:
                    if isinstance(X, int) and X == 5 and t < 2:
                        act.wait_ge(roped, 25 * (L + 1))
                    if not (isinstance(X, int) and X == 5 and t < 2 and L == 0):
                        act.wait_ge(s_zout[t % 2], (X - 5) * (16 * Z_STORES[t % 2]) + (64 * Z_STORES[t % 2] * L + 16 * (t // 2)))
                    dst, src = (t1, t2)[t % 2][:, :], src[:, :]
                s.copy(dst, src).then_inc(tr_free, 1)

            def h_evacuate(L, kt):
                act.wait_ge(h_tr, KT * L + kt + 1)
                if kt >= 2:
                    act.wait_ge(h_ready, H0[L] + kt - 1)
                elif kt == 0:
                    act.wait_ge(ab_ready, L + 1)
                    act.wait_ge(*((xsq_done, 1) if L == 0 else (xsq_l1, 20 + TT)))
                s.activation(h32[:, kt % 2, 0:NC], bank[6][:, :], ACT.Identity,
                             bias=addB[:, kt, 0:1], scale=mulA[:, kt, 0:1])
                s.activation(h32[:, kt % 2, NC:NC + P], bank[7][:, 0:P], ACT.Identity,
                             bias=addB[:, kt, 1:2], scale=mulA[:, kt, 1:2]).then_inc(h_ev, 1)

            def gated_hi(L, kt):
                src = qT[:, kt // 4, :, (kt % 4) * P:(kt % 4 + 1) * P]
                s.copy(hT_hi[:, kt, :].rearrange("p (t n) -> p t n", t=TT), src).then_inc(h_ev, 1)

            def chunk(L, ch, kind, X, mod=None):
                split_hi(L, ch, 0)
                if kind in ("k", "v", "q", "z"):
                    evacuate(L, ch, kind, X)
                split_hi(L, ch, 1)
                if kind in ("k", "q"):
                    head_squares(L, X)
                for p in range(2, PAIRS):
                    split_hi(L, ch, p)
                    if kind in ("k", "q", "z") and p - 2 < TT:
                        evac_transposed(L, kind, X, p - 2)
                    if kind == "v" and p == 3:
                        act.wait_ge(tr_done, N_TR * L + TT + 1)
                        s.copy(kT[:, :, CTX:CTX + P], bank[7][:, :].rearrange("p (g n) -> p g n", g=4)
                               ).then_inc(tr_free, 1)
                    if kind == "o" and L == 0 and p - 2 < TT:
                        new_square(ch - FIRST_O - 1, p - 2)
                if mod is not None:
                    mod_evacuate(mod_used, mod[0] * PAIRS + PAIRS, mod[1])

            def new_square(n, t):
                act.wait_ge(x_new, n * TT + (t + 1))
                s.activation(stage[:, t, :], x_tok[:, t, ds(n * NC, NC)], ACT.Square,
                             accum_out=ss_x[:, t, ds(n, 1)]).then_inc(xsq_l1, 1)

            for L in range(LAYERS):
                split_hi(L, 0, 0)
                act.wait_ge(x_summed, L + 1)
                if L == 0:
                    act.wait_ge(const_made, 1)
                s.activation(rms_x[:, :], sum_x[:, :], ACT.Sqrt, bias=eps[:, :], scale=1.0 / D).then_inc(x_rooted, 1)
                for p in range(PAIRS):
                    if p:
                        split_hi(L, 0, p)
                    for kt in (2 * p, 2 * p + 1):
                        h_evacuate(L, kt)
                mod_evacuate(mod_used, PAIRS * (6 * L + 1), 4 + 6 * L)
                chunk(L, 1, "k", 0, (6 * L + 1, 5 + 6 * L))
                chunk(L, 2, "v", None, (2, 6) if L == 0 else None)
                act.wait_ge(s_newk, 16 * (L + 1))
                with act.Fori(1, 4) as i:
                    chain.enter(i, 1, 4 * TT)
                    chunk(L, i + 2, "q", i, (i + 2, i + 6) if L == 0 else None)
                    chain.leave(4)
                chunk(L, FIRST_Z, "q", 4)
                with act.Fori(1, 4) as i:
                    chunk(L, i + FIRST_Z, "z", i + 4)
                evacuate(L, FIRST_O, "z", 8)
                for t in range(TT):
                    evac_transposed(L, "z", 8, t)

                def exps(gg, u, h):
                    U, prev = unit(L, gg, u), same_buffer(L, gg, u)
                    b, n = buf(u), P * n_kt[L][u]
                    if h == 0:
                        act.wait_ge(nm_ready, U + 1)
                        act.wait_ge(o_done, prev + (CREDIT + 1))
                    m = min(n, NC)
                    ins = s.activation(probs[b][:, h, 0:m], bank[h][:, 0:m], ACT.Exp, bias=nmax[:, h:h + 1],
                                       scale=SCALE, accum_out=den[:, h:h + 1])
                    if n > NC:
                        ins = s.activation(probs[b][:, h, NC:n], bank[4][:, h * P:(h + 1) * P], ACT.Exp,
                                           bias=nmax[:, h:h + 1], scale=SCALE, accum_out=denx[:, h:h + 1])
                    if L == 0 and h == 3:
                        ins = s.activation(denx[:, :], sinkd[:, :], ACT.Exp)
                    ins.then_inc(exp_done, 1)

                def probs_out(gg, u, kt):
                    U, prev = unit(L, gg, u), same_buffer(L, gg, u)
                    act.wait_ge(pt_done, before(n_kt, L, gg, u) + (kt + 1))
                    if kt == 0:
                        act.wait_ge(o_done, prev + (CREDIT + 1))
                    s.copy(probsT[buf(u)][:, kt, :], bank[5 + kt % 2][:, :]).then_inc(pt_act, 1)

                def act_group(gg, last):
                    for u in range(TT):
                        even = list(range(0, n_kt[L][u], 2))
                        ng, nu = (gg, u + 1) if u < TOK else (gg + 1, 0)
                        for h in range(4):
                            if not (last and u == TOK):
                                exps(ng, nu, h)
                            if even:
                                probs_out(gg, u, even.pop(0))
                        assert not even

                for h in range(4):
                    exps(0, 0, h)
                with act.Fori(0, 3) as gg:
                    act_group(gg, False)
                act_group(3, True)

                split_hi(L, FIRST_O, 0)
                for p in range(PAIRS):
                    if p:
                        split_hi(L, FIRST_O, p)
                    for kt in (2 * p, 2 * p + 1):
                        if kt == 0:
                            act.wait_ge(gated, CREDIT + 20 * (L + 1))
                            act.wait_ge(o_done, CREDIT + 20 * (L + 1))
                        gated_hi(L, kt)
                with act.Fori(1, 4) as n:
                    chunk(L, n + FIRST_O, "o", None)
                if L == 0:
                    for t in range(TT):
                        new_square(3, t)

        @block.vector
        def _(dve):
            chain = Chain(dve_chain)
            v = nc.vector
            dve.wait_ge(s_sink, 16)
            chain.link(dve, v.tensor_scalar(neg_sink[:, :], sink[:, :], -1.0, None, ALU.mult))
            dve.wait_ge(consts_T, 1)
            v.tensor_copy(consts[:, :], bank[7][:, 0:P]).then_inc(consts_ready, 1)

            def x_norm(L):
                if L == 0:
                    dve.wait_ge(xsq_done, 1)
                    dve.wait_ge(s_x, 16 * TT)
                else:
                    dve.wait_ge(xsq_l1, 20 + TT)
                v.tensor_reduce(sum_x[:, :], ss_x[:, :, :], AX, ALU.add).then_inc(x_summed, 1)
                dve.wait_ge(x_rooted, L + 1)
                chain.link(dve, v.reciprocal(r_x[:, :], rms_x[:, :]))
                for n in range(4):
                    if L == 1 and n == 0:
                        dve.wait_ge(s_y, 16 * TT * 4)
                    for t in range(TT):
                        ins = v.tensor_scalar(x_tok[:, t, n * NC:(n + 1) * NC], x_tok[:, t, n * NC:(n + 1) * NC],
                                              r_x[:, t:t + 1], None, ALU.mult)
                    ins.then_inc(x_normed, 1)

            def scale_shift(L):
                dve.wait_ge(modT_done, L + 1)
                src = bank[7][:, 0:64].rearrange("p (r j) -> p j r", r=2)
                bias = consts[:, 64 + 32 * L:96 + 32 * L]

                def both(a):
                    return a.rearrange("p (k r) -> p k r", r=1).to_broadcast([P, KT, 2])

                if L == 1:
                    dve.wait_ge(h_ready, H0[0] + KT)
                v.tensor_tensor(addB[:, :, :], src[:, 0:KT, :], both(bias[:, 0:KT]), ALU.add)
                chain.link(dve, v.tensor_tensor(mulA[:, :, :], src[:, KT:2 * KT, :], both(bias[:, KT:2 * KT]), ALU.add))
                v.scalar_tensor_tensor(mulA[:, :, :], mulA[:, :, :], 1.0,
                                       both(consts[:, 32 + 16 * L:48 + 16 * L]), ALU.add, ALU.mult
                                       ).then_inc(ab_ready, 1)

            def tables(n):
                dve.wait_ge(s_tab, 48 * (n + 1))
                gb = gain[:, :].rearrange("p (t d) -> p t d", t=1).to_broadcast([P, TOK, P])
                chain.link(dve, v.tensor_tensor(rope_c[:, :, :], rope_c[:, :, :], gb, ALU.mult))
                for a in range(2):
                    for hf in range(2):
                        o, other = 64 * a + 32 * hf, 64 * a + 32 * (1 - hf)
                        gs = gain[:, other:other + 32].rearrange("p (t d) -> p t d", t=1).to_broadcast([P, TOK, 32])
                        ins = v.tensor_tensor(rope_s[:, :, o:o + 32], rope_s[:, :, o:o + 32], gs, ALU.mult)
                chain.link(dve, ins)

            def split_lo(L, ch, p):
                C = ch + 14 * L
                dve.wait_ge(whi_ready, C * PAIRS + (p + 1))
                dve.wait_ge(s_w[p % 2], C * 64 + 16 * (p // 2 + 1))
                v.tensor_tensor(w_lo[:, p % 2], w_raw[:, p % 2], w_hi[:, p % 2].bitcast(f32),
                                ALU.subtract).then_inc(wlo_ready, 1)

            def norm_rope(L, X, t):
                R = X * TT + (25 * L + t)
                dve.wait_ge(ss_ready, R + 1)
                chain.link(dve, v.reciprocal(r_h[:, :], rms_h[:, t, :]))
                st = stage[:, t, :].rearrange("p (h d) -> p h d", h=4)
                rb = r_h[:, :].rearrange("p (h d) -> p h d", d=1).to_broadcast([P, 4, P])
                chain.link(dve, v.tensor_tensor(st, st, rb, ALU.mult))
                if t == TOK:
                    gb = gain[:, :].rearrange("p (h d) -> p h d", h=1).to_broadcast([P, 4, P])
                    v.tensor_tensor(st, st, gb, ALU.mult).then_inc(roped, 1)
                    dve.wait_ge(roped, R + 1)
                    return
                a1 = t1[:, :].rearrange("p (h d) -> p h d", h=4)
                a2 = t2[:, :].rearrange("p (ha f d) -> p ha f d", f=2, d=32)
                sf = stage[:, t, :].rearrange("p (ha f d) -> p ha f d", f=2, d=32)
                cb = rope_c[:, t:t + 1, :].to_broadcast([P, 4, P])
                v.tensor_tensor(a1, st, cb, ALU.mult)
                for hf in range(2):
                    for a in range(2):
                        o = 64 * a + 32 * hf
                        x_other = stage[:, t, :].rearrange("p (h d) -> p h d", h=4)[:, :, 64 * a + 32 * (1 - hf):64 * a + 32 * (1 - hf) + 32]
                        dst = t2[:, :].rearrange("p (h d) -> p h d", h=4)[:, :, o:o + 32]
                        ins = v.tensor_tensor(dst, x_other, rope_s[:, t:t + 1, o:o + 32].to_broadcast([P, 4, 32]), ALU.mult)
                chain.link(dve, ins)
                v.tensor_tensor(stage[:, t, :], t1[:, :], t2[:, :], ALU.add).then_inc(roped, 1)
                dve.wait_ge(roped, R + 1)

            LINKS_Q = 2 * TT + TOK

            def gate_add(L, n):
                dve.wait_ge(s_old, (n * 128 + 128 * (4 * L + 1)) if not isinstance(n, int) else 128 * (4 * L + n + 1))
                for_both = gate_b.rearrange("p (r n) -> p r n", r=1).to_broadcast([P, 2, NC])
                chain.link(dve, v.tensor_tensor(gate, gate, for_both, ALU.add))

            def gate_out(L, n, t):
                dve.wait_ge(acc_done, n * TT + (TT * (14 * L + FIRST_O) + t + 1))
                if L == 0:
                    dve.wait_ge(xsq_l1, n * TT + (t + 1))
                v.tensor_tensor(stage[:, t, :], bank[t][:, :], gate[:, 0 if t < TOK else 1, :],
                                ALU.mult).then_inc(acc_free, 1)

            def add_x(L, n, t):
                dve.wait_ge(acc_free, n * TT + (TT * (14 * L + FIRST_O) + t + 1))
                v.tensor_tensor(x_tok[:, t, ds(n * NC, NC)], stage[:, t, :], x_old[:, t, :],
                                ALU.add).then_inc(x_new, 1)

            def chunk(L, ch, kind, X):
                split_lo(L, ch, 0)
                if kind == "o":
                    gate_add(L, ch - FIRST_O - 1)
                    for t in range(TT):
                        gate_out(L, ch - FIRST_O - 1, t)
                split_lo(L, ch, 1)
                for p in range(2, PAIRS):
                    if p - 2 < TT:
                        if kind in ("k", "q"):
                            norm_rope(L, X, p - 2)
                        if kind == "o":
                            add_x(L, ch - FIRST_O - 1, p - 2)
                    split_lo(L, ch, p)

            tables(0)
            for L in range(LAYERS):
                if L == 0:
                    x_norm(0)
                    dve.wait_ge(consts_ready, 1)
                    scale_shift(0)
                split_lo(L, 0, 0)
                if L == 1:
                    x_norm(1)
                    dve.wait_ge(acc_done, 14 * TT)
                for p in range(PAIRS):
                    if p:
                        split_lo(L, 0, p)
                    for kt in (2 * p, 2 * p + 1):
                        dve.wait_ge(h_ev, H0[L] + kt + 1)
                        if kt == 0 and L == 0:
                            dve.wait_ge(first_used, 4 * PAIRS)
                        chain.link(dve, v.tensor_copy(hT_hi[:, kt, :], h32[:, kt % 2, :]))
                        v.tensor_tensor(hT_lo[:, kt, :], h32[:, kt % 2, :], hT_hi[:, kt, :].bitcast(f32),
                                        ALU.subtract).then_inc(h_ready, 1)
                chunk(L, 1, "k", 0)
                split_lo(L, 2, 0)
                split_lo(L, 2, 1)
                tables(2 * L + 1)
                for p in range(2, PAIRS):
                    split_lo(L, 2, p)
                with dve.Fori(1, 4) as i:
                    chain.enter(i, 1, LINKS_Q)
                    chunk(L, i + 2, "q", i)
                    chain.leave(4)
                chunk(L, FIRST_Z, "q", 4)
                with dve.Fori(1, 4) as i:
                    chunk(L, i + FIRST_Z, None, None)
                if L == 0:
                    tables(2)

                def maxima(gg, u):
                    U = unit(L, gg, u)
                    n = P * n_kt[L][u]
                    if n > NC:
                        dve.wait_ge(scx_done, gg * TOK + (u + 1))
                        v.tensor_reduce(mxc[:, :], bank[4][:, :].rearrange("p (h k) -> p h k", h=4), AX, ALU.max)
                    for h in range(4):
                        dve.wait_ge(sc_done, U * 4 + (4 * CREDIT + h + 1))
                        ins = v.tensor_reduce(mx[:, h:h + 1], bank[h][:, 0:min(n, NC)], AX, ALU.max)
                    chain.link(dve, ins)
                    if n > NC:
                        chain.link(dve, v.tensor_tensor(mx[:, :], mx[:, :], mxc[:, :], ALU.max))
                    if L == 1:
                        v.tensor_scalar(nmax[:, :], mx[:, :], -SCALE, None, ALU.mult).then_inc(nm_ready, 1)
                    else:
                        chain.link(dve, v.scalar_tensor_tensor(nmax[:, :], mx[:, :], -SCALE, neg_sink[:, ds(gg * 4, 4)],
                                                               ALU.mult, ALU.min))
                        v.tensor_tensor(sinkd[:, :], nmax[:, :], sink[:, ds(gg * 4, 4)], ALU.add).then_inc(nm_ready, 1)

                def normalise(gg, u):
                    U, b, n = unit(L, gg, u), buf(u), P * n_kt[L][u]
                    dve.wait_ge(exp_done, U * 4 + 8)
                    if L == 0 or n > NC:
                        chain.link(dve, v.tensor_tensor(rden[:, :], den[:, :], denx[:, :], ALU.add))
                        chain.link(dve, v.reciprocal(rden[:, :], rden[:, :]))
                    else:
                        chain.link(dve, v.reciprocal(rden[:, :], den[:, :]))
                    for h in range(4):
                        ins = v.tensor_scalar(probs[b][:, h, 0:n], probs[b][:, h, 0:n], rden[:, h:h + 1], None, ALU.mult)
                    ins.then_inc(pn_ready, 1)

                def probs_out(gg, u, kt):
                    U, prev = unit(L, gg, u), same_buffer(L, gg, u)
                    dve.wait_ge(pt_done, before(n_kt, L, gg, u) + (kt + 1))
                    if kt == 1:
                        dve.wait_ge(o_done, prev + (CREDIT + 1))
                    v.tensor_copy(probsT[buf(u)][:, kt, :], bank[5 + kt % 2][:, :]).then_inc(pt_dve, 1)

                def gate_unit(gg, u):
                    U = unit(L, gg, u)
                    dve.wait_ge(o_done, U + (CREDIT + 1))
                    dve.wait_ge(s_zin[u], gg * 16 + 16 * (4 * L + 1))
                    dve.wait_ge(q_split, U + 1)
                    dst = qT[:, ds(gg, 1), u, :].rearrange("p g n -> p (g n)")
                    v.tensor_tensor(dst, bank[7][:, :], z_in[:, u, :], ALU.mult).then_inc(gated, 1)

                def dve_group(gg, last):
                    for u in range(TT):
                        normalise(gg, u)
                        odd = list(range(1, n_kt[L][u], 2))
                        if u < TOK:
                            maxima(gg, u + 1)
                        elif not last:
                            maxima(gg + 1, 0)
                        for kt in odd:
                            probs_out(gg, u, kt)
                        gate_unit(gg, u)

                maxima(0, 0)
                per = (TT * 2 + TT * 2) if L == 0 else (TOK * 2 + 1) + (TOK * 2 + 1)
                with dve.Fori(0, 3) as gg:
                    chain.enter(gg, 0, per)
                    dve_group(gg, False)
                    chain.leave(3)
                dve_group(3, True)

                split_lo(L, FIRST_O, 0)
                for p in range(PAIRS):
                    if p:
                        split_lo(L, FIRST_O, p)
                    for kt in (2 * p, 2 * p + 1):
                        dve.wait_ge(h_ev, H0[L] + KT + kt + 1)
                        src = qT[:, kt // 4, :, (kt % 4) * P:(kt % 4 + 1) * P]
                        v.tensor_tensor(hT_lo[:, kt, :].rearrange("p (t n) -> p t n", t=TT), src,
                                        hT_hi[:, kt, :].bitcast(f32).rearrange("p (t n) -> p t n", t=TT),
                                        ALU.subtract).then_inc(h_ready, 1)
                if L == 0:
                    scale_shift(1)
                dve.wait_ge(h_ready, H0[L] + 2 * KT)
                with dve.Fori(1, 4) as n:
                    chain.enter(n, 1, 1)
                    chunk(L, n + FIRST_O, "o", None)
                    chain.leave(4)
                gate_add(L, 3)
                for t in range(TT):
                    gate_out(L, 3, t)
                for t in range(TT):
                    add_x(L, 3, t)
        @block.tensor
        def _(pe):
            mm = nc.tensor.matmul
            pe.sem_inc(o_done, CREDIT)
            pe.sem_inc(gated, CREDIT)
            pe.sem_inc(sc_done, 4 * CREDIT)
            pe.sem_inc(exp_done, 4)
            pe.sem_inc(xsq_l1, TT)
            pe.sem_inc(pt_act, 1)
            pe.sem_inc(pt_dve, 1)
            pe.wait_ge(const_made, 1)
            pe.wait_ge(s_rows, 80)
            nc.tensor.transpose(bank[7][:, 0:P], rows[:, :], ident[:, :]).then_inc(consts_T, 1)
            pe.wait_ge(cond_ready, 1)

            def mod_products(w, s, used):
                for kk in range(2):
                    k = 2 * s + kk
                    for j in range(4):
                        ins = mm(bank[MODBANK][32 * j:32 * j + 2, 0:256], cond[:, k, :], w[:, kk, j * 256:(j + 1) * 256],
                                 start=(k == 0), stop=(k == KT - 1))
                ins.then_inc(used, 1)

            def first_block(b, wait):
                if wait:
                    pe.wait_ge(mod_evac, b)
                for s in range(PAIRS):
                    pe.wait_ge(s_first[s], b * 16 + 16)
                    mod_products(first_ring[:, s], s, first_used)

            first_block(0, False)
            with pe.Fori(1, 4) as b:
                first_block(b, True)

            def mod_rows_T(L):
                pe.wait_ge(s_modin, 32 * (L + 1))
                if L == 0:
                    pe.wait_ge(consts_ready, 1)
                nc.tensor.transpose(bank[7][:, 0:64], rows[0:64, :], ident[0:64, 0:64]).then_inc(modT_done, 1)

            def chunk(L, ch, kind, X, mod=None, fresh=None):
                C = ch + 14 * L
                start = isinstance(ch, int) and ch == 0 and L == 0
                for p in range(PAIRS):
                    pe.wait_ge(wlo_ready, C * PAIRS + (p + 1))
                    for kk in range(2):
                        k = 2 * p + kk
                        if fresh == "x":
                            for kt in ((0, 1, 2) if k == 0 else (k + 2,)):
                                if kt < KT:
                                    h_transposes(L, kt)
                        if fresh is not None:
                            pe.wait_ge(h_ready, H0[L] + (KT if fresh == "o" else 0) + k + 1)
                        for t in range(TT):
                            if k == 0 and not start:
                                pe.wait_ge(acc_free, C * TT + (t - 4))
                            hi, lo = hT_hi[:, k, t * P:(t + 1) * P], hT_lo[:, k, t * P:(t + 1) * P]
                            mm(bank[t][:, :], hi, w_hi[:, p % 2, kk], start=(k == 0), stop=False)
                            mm(bank[t][:, :], hi, w_lo[:, p % 2, kk], start=False, stop=False)
                            ins = mm(bank[t][:, :], lo, w_hi[:, p % 2, kk], start=False, stop=(k == KT - 1))
                            if k == KT - 1:
                                ins.then_inc(acc_done, 1)
                    if p < PAIRS - 1:
                        ins.then_inc(mm_done, 1)
                    if mod is not None:
                        if p == 0:
                            pe.wait_ge(mod_evac, mod[1])
                        pe.wait_ge(s_mw[p % 2], mod[0] * 64 + 16 * (p // 2 + 1))
                        mod_products(mod_w[:, p % 2], p, mod_used)
                    if kind in ("k", "q", "z") and 1 <= p <= TT:
                        stage_transposes(L, kind, X, p - 1)
                    if kind == "v" and p == 2:
                        pe.wait_ge(s_ck, 16 * (L + 1))
                        pe.wait_ge(tr_free, N_TR * L + TT)
                        for h in range(4):
                            ins = nc.tensor.transpose(bank[7][:, h * P:(h + 1) * P], stage[:, 0, h * P:(h + 1) * P], ident[:, :])
                        ins.then_inc(tr_done, 1)

            def h_transposes(L, kt):
                if kt % 4 == 0:
                    pe.wait_ge(x_normed, 4 * L + kt // 4 + 1)
                if kt > 0:
                    pe.wait_ge(h_ev, H0[L] + kt)
                else:
                    pe.wait_ge(ab_ready, L + 1)
                for t in range(TT):
                    dst = bank[6][:, t * P:(t + 1) * P] if t < TOK else bank[7][:, 0:P]
                    ins = nc.tensor.transpose(dst, x_tok[:, t, kt * P:(kt + 1) * P], ident[:, :])
                ins.then_inc(h_tr, 1)

            def stage_transposes(L, kind, X, t):
                n = tr_number(L, X, t)
                if kind == "z":
                    pe.wait_ge(acc_free, (X - 5) * TT + (TT * (14 * L + FIRST_Z) + t + 1))
                else:
                    pe.wait_ge(roped, X * TT + (25 * L + t + 1))
                if isinstance(X, int) and X == 0 and t == 0:
                    pe.wait_ge(h_ev, H0[L] + KT)
                elif t == 0:
                    pe.wait_ge(tr_free, n)
                elif not (isinstance(n, int) and n == 1):
                    pe.wait_ge(tr_free, n - 1)
                for h in range(4):
                    ins = nc.tensor.transpose(bank[6 + t % 2][:, h * P:(h + 1) * P], stage[:, t, h * P:(h + 1) * P], ident[:, :])
                ins.then_inc(tr_done, 1)

            mod_rows_T(0)
            for L in range(LAYERS):
                chunk(L, 0, None, None, (6 * L, 4 + 6 * L), fresh="x")
                chunk(L, 1, "k", 0, (6 * L + 1, 5 + 6 * L))
                chunk(L, 2, "v", None, (2, 6) if L == 0 else None)
                with pe.Fori(1, 4) as i:
                    chunk(L, i + 2, "q", i, (i + 2, i + 6) if L == 0 else None)
                chunk(L, FIRST_Z, "q", 4)
                with pe.Fori(1, 4) as i:
                    chunk(L, i + FIRST_Z, "z", i + 4)

                def scores(gg, u):
                    U, b = unit(L, gg, u), buf(u)
                    pe.wait_ge(q_split, U + 1)
                    if u == 0:
                        pe.wait_ge(kv_main, gg * 2 + (8 * L + 1))
                    if u == TOK:
                        pe.wait_ge(kv_req, gg * 2 + (8 * L + 1))

                    def product(out, h, col, n, stop=True):
                        q = slice(h * P, (h + 1) * P)
                        mm(out, q_hi[b][:, q], k_hi[:, col:col + n], start=True, stop=False)
                        mm(out, q_hi[b][:, q], k_lo[:, col:col + n], start=False, stop=False)
                        return mm(out, q_lo[b][:, q], k_hi[:, col:col + n], start=False, stop=stop)

                    if L == 1 and u < TOK:
                        pe.wait_ge(exp_done, U * 4 + 4)
                        for h in range(4):
                            ins = product(bank[4][:, h * P:(h + 1) * P], h, CTX, P)
                        ins.then_inc(scx_done, 1)
                    parts = key_parts(L, u)
                    masks = []
                    if L == 0 and 0 < u < TOK:
                        masks.append((0, mask_prev))
                    if L == 0 and u < TOK - 1:
                        masks.append((P if u == 0 else 2 * P, mask_next))
                    for h in range(4):
                        pe.wait_ge(exp_done, U * 4 + (h + 1))
                        if len(parts) == 2:
                            product(bank[h][:, parts[0][1]:parts[0][1] + P], h, parts[1][0], P)
                        ins = product(bank[h][:, 0:parts[0][1]], h, *parts[0], stop=not masks)
                        for n, (at, mask) in enumerate(masks):
                            ins = mm(bank[h][:, at:at + P], ident_b[:, :], mask[:, :], start=False,
                                     stop=(n == len(masks) - 1))
                        ins.then_inc(sc_done, 1)

                def values(gg, u):
                    U, b, tiles = unit(L, gg, u), buf(u), key_tiles(L, u)
                    pe.wait_ge(pn_ready, U + 1)
                    if u == 0:
                        pe.wait_ge(kv_main, gg * 2 + (8 * L + 2))
                    if u == TOK:
                        pe.wait_ge(kv_req, gg * 2 + (8 * L + 2))

                    def probs_T(kt):
                        table, done = (n_even, pt_act) if kt % 2 == 0 else (n_odd, pt_dve)
                        pe.wait_ge(done, before(table, L, gg, u) + (kt // 2 + 1))
                        for h in range(4):
                            ins = nc.tensor.transpose(bank[5 + kt % 2][:, h * P:(h + 1) * P],
                                                      probs[b][:, h, kt * P:(kt + 1) * P], ident[:, :])
                        ins.then_inc(pt_done, 1)

                    probs_T(0)
                    for kt, vt in enumerate(tiles):
                        if kt + 1 < len(tiles):
                            probs_T(kt + 1)
                        if kt % 2 == 0:
                            pe.wait_ge(pt_act, before(n_even, L, gg, u) + (kt // 2 + 2))
                        else:
                            pe.wait_ge(pt_dve, before(n_odd, L, gg, u) + (kt // 2 + 2))
                        if kt == 0:
                            pe.wait_ge(gated, U + CREDIT)
                        ins = mm(bank[7][:, :], v_g[:, vt, :], probsT[b][:, kt, :], start=(kt == 0),
                                 stop=(kt == len(tiles) - 1))
                    ins.then_inc(o_done, 1)

                def pe_group(gg, last):
                    for u in range(TT):
                        if u < TOK:
                            scores(gg, u + 1)
                        elif not last:
                            scores(gg + 1, 0)
                        values(gg, u)

                pe.wait_ge(acc_free, TT * (14 * L + FIRST_O))
                for t in range(TT):
                    stage_transposes(L, "z", 8, t)
                scores(0, 0)
                pe.wait_ge(tr_free, N_TR * (L + 1))
                pe.wait_ge(mod_evac, 10 + 2 * L)
                with pe.Fori(0, 3) as gg:
                    pe_group(gg, False)
                pe_group(3, True)

                chunk(L, FIRST_O, None, None, fresh="o")
                if L == 0:
                    mod_rows_T(1)
                with pe.Fori(1, 4) as n:
                    chunk(L, n + FIRST_O, None, None)


def rope_tables():
    n_tokens, grid_w, n_freq, theta = 512, 64, 32, 10000.0
    row, col = np.arange(n_tokens) // grid_w, np.arange(n_tokens) % grid_w
    inv = (np.float32(theta) ** (-np.arange(n_freq, dtype=np.float32) / n_freq)).astype(np.float32)
    ang = np.stack([row.astype(np.float32)[:, None] * inv, col.astype(np.float32)[:, None] * inv], axis=1)
    cos, sin = np.cos(ang).astype(np.float32), np.sin(ang).astype(np.float32)
    full_cos = np.stack([cos, cos], axis=2).reshape(n_tokens, 128)
    full_sin = np.stack([-sin, sin], axis=2).reshape(n_tokens, 128)
    return np.ascontiguousarray(full_cos), np.ascontiguousarray(full_sin)


_INS = ["x_prompt", "x_sample", "c", "cache_k", "cache_v", "c_ctx", "norm_g", "w_mod", "b_mod", "w_in",
        "q_norm_g", "k_norm_g", "sinks", "w_out"]
_OUTS = [("y_prompt", (1, 128, 2048)), ("y_sample", (1, 512, 2048)),
         ("new_cache_k", (1, 2, 128, 4, 128)), ("new_cache_v", (1, 2, 128, 4, 128))]


def kernel(**inputs):
    import concourse.bacc as bacc
    from concourse.bass_utils import run_bass_kernel_spmd

    nc = bacc.Bacc("TRN2", target_bir_lowering=False, num_devices=1)
    arrays = {f"in_{n}": np.ascontiguousarray(inputs[n]) for n in _INS}
    arrays["in_rope_cos"], arrays["in_rope_sin"] = rope_tables()
    args = [nc.dram_tensor(n, a.shape, mybir.dt.from_np(a.dtype), kind="ExternalInput").ap()
            for n, a in arrays.items()]
    args += [nc.dram_tensor(f"out_{n}", s, mybir.dt.float32, kind="ExternalOutput").ap() for n, s in _OUTS]
    build(nc, *args)
    r = run_bass_kernel_spmd(nc, [arrays], core_ids=[0])
    return tuple(r.results[0][f"out_{n}"] for n, _ in _OUTS)
```

```python
import numpy as np
import concourse.bass as bass
from concourse import mybir
from contextlib import ExitStack

P = 128
D = 2048
KT = D // P
TOK = 4
TT = TOK + 1
HEADS, KVH, GROUP = 16, 4, 4
NC = 512
PROJ = 5120
PAIRS = KT // 2
LAYERS = 2
N_CHUNKS = 14
FIRST_Z, FIRST_O = 6, 10
MODB = 1024
HALF = MODB // 2
GROUPS = D // HALF
PER = KT // GROUPS
RING0 = 7
EPS = 1e-6
SCALE = P ** -0.5
NEG = -1e30
CTX, REQ = TOK * P, TT * P
KCOLS = 6 * P
CREDIT = 5
N_TR = 46


def build(nc, x_prompt, x_sample, c, cache_k, cache_v, c_ctx, norm_g, w_mod, b_mod, w_in, q_norm_g,
          k_norm_g, sinks, w_out, rope_cos, rope_sin, y_prompt, y_sample, new_k, new_v):
    f32, f32r, bf16 = mybir.dt.float32, mybir.dt.float32r, mybir.dt.bfloat16
    ALU, ACT, AX = mybir.AluOpType, mybir.ActivationFunctionType, mybir.AxisListType.X
    ds = bass.ds
    ctx = ExitStack()
    with ctx:
        def sb(name, shape, dt=f32):
            return ctx.enter_context(nc.sbuf_tensor(name, shape, dt))

        def sem(name):
            return ctx.enter_context(nc.semaphore(name))

        gate_rows = nc.dram_tensor("gate_rows", [2, LAYERS * D], f32, kind="Internal").ap()
        z_spill = nc.dram_tensor("z_spill", [KVH, TT, P, NC], f32, kind="Internal").ap()
        x_spill = nc.dram_tensor("x_spill", [TT, P, D], f32, kind="Internal").ap()

        def phase(*tensors):
            with ExitStack() as shared:
                return [shared.enter_context(nc.sbuf_tensor(*t)) for t in tensors]

        region = ("region", [P, 2 * KT * TT * P], f32)
        hT_hi, hT_lo = phase(*[(f"hT_{n}", [P, KT, TT * P], f32r) for n in ("hi", "lo")])
        tail = 12 * TT * P
        _, slot5, _, slot6 = phase(("pad0", [P, tail], f32), ("slot5", [P, 2, MODB], f32),
                                   ("pad1", [P, KT * TT * P - 2 * MODB], f32), ("slot6", [P, 2, MODB], f32))
        a = phase(("probs0", [P, 4, 5 * P], f32), ("probs1", [P, 4, 5 * P], f32), ("probs2", [P, 4, P], f32),
                  ("probsT0", [P, 5, NC], f32), ("probsT1", [P, 5, NC], f32), ("probsT2", [P, 1, NC], f32),
                  ("z_in", [P, TT, NC], f32), ("v_g", [P, 6, P], f32),
                  ("k_hi", [P, KCOLS], f32r), ("k_lo", [P, KCOLS], f32r),
                  *[(f"q_{n}{b}", [P, NC], f32r) for n in ("hi", "lo") for b in range(3)])
        probs, probsT, (z_in, v_g, k_hi, k_lo), q_hi, q_lo = a[0:3], a[3:6], a[6:10], a[10:13], a[13:16]
        ctx.enter_context(nc.sbuf_tensor(*region))

        qT_x = sb("qT_x", [P, KVH * TT * NC])
        qT = qT_x[:, :].rearrange("p (g t n) -> p g t n", g=KVH, t=TT)
        x_tok = qT_x[:, :].rearrange("p (t n) -> p t n", t=TT)
        kv = sb("kv", [P, 2 * KVH * KCOLS])
        kT = kv[:, 0:KVH * KCOLS].rearrange("p (g k) -> p g k", g=KVH)
        v_tok = kv[:, KVH * KCOLS:].rearrange("p (t n) -> p t n", t=6)
        w_raw = sb("w_raw", [P, 2, 2, NC])
        w_hi = sb("w_hi", [P, 2, 2, NC], f32r)
        w_lo = sb("w_lo", [P, 2, 2, NC], f32r)
        mod_ring = sb("mod_ring", [P, 2 * 2048])
        mod_w = mod_ring[:, :].rearrange("p (s k n) -> p s k n", s=2, k=2)
        first_ring = [kv[:, i * 2 * MODB:(i + 1) * 2 * MODB].rearrange("p (k n) -> p k n", k=2) for i in range(3)]
        first_ring += [mod_w[:, 0], mod_w[:, 1], slot5[:, :, :], slot6[:, :, :]]
        x_old = mod_ring[:, 0:TT * NC].rearrange("p (t n) -> p t n", t=TT)
        gate = mod_ring[:, 2560:3584].rearrange("p (r n) -> p r n", r=2)
        gate_b = mod_ring[:, 3584:4096]
        stage = sb("stage", [P, TT, NC])
        h32 = stage[:, :, :].rearrange("p t n -> p (t n)")[:, 0:2 * TT * P].rearrange("p (s n) -> p s n", s=2)
        t1, t2 = sb("t1", [P, NC]), sb("t2", [P, NC])
        rope_c, rope_s = sb("rope_c", [P, TOK, P]), sb("rope_s", [P, TOK, P])
        gain = sb("gain", [P, P])
        mod_ev = sb("mod_ev", [P, MODB // 4])
        ident = sb("ident", [P, P])
        ident_b, mask_prev, mask_next = (sb(n, [P, P], bf16) for n in ("ident_b", "mask_prev", "mask_next"))
        consts = sb("consts", [P, P])
        rows = sb("rows", [P, P])
        cond = sb("cond", [P, KT, 2])
        mulA, addB = sb("mulA", [P, KT, 2]), sb("addB", [P, KT, 2])
        junk, eps = sb("junk", [P, P]), sb("eps", [P, 1])
        ss_x, ss_h = sb("ss_x", [P, TT, 4]), sb("ss_h", [P, TT, 4])
        rms_x, rms_h = sb("rms_x", [P, TT]), sb("rms_h", [P, TT, 4])
        sum_x, r_x, r_h = sb("sum_x", [P, TT]), sb("r_x", [P, TT]), sb("r_h", [P, 4])
        sink, neg_sink = sb("sink", [P, HEADS]), sb("neg_sink", [P, HEADS])
        mx, mxc, nmax, den, denx, sinkd, rden = (sb(n, [P, 4]) for n in
                                                 ("mx", "mxc", "nmax", "den", "denx", "sinkd", "rden"))
        bank = [ctx.enter_context(nc.psum_tensor(f"bank{i}", [P, 512], f32)) for i in range(8)]
        MODBANK = 5

        s_rows, s_x, s_sink = sem("s_rows"), sem("s_x"), sem("s_sink")
        s_first = [sem(f"s_first{i}") for i in range(RING0)]
        s_w = [sem(f"s_w{i}") for i in range(2)]
        s_mw = [sem(f"s_mw{i}") for i in range(2)]
        s_gate, s_tab, s_ck, s_cv, s_y3 = (sem(n) for n in ("s_gate", "s_tab", "s_ck", "s_cv", "s_y3"))
        s_newk, s_newv, s_y = sem("s_newk"), sem("s_newv"), sem("s_y")
        s_zout, s_zin = [sem(f"s_zout{i}") for i in range(2)], [sem(f"s_zin{i}") for i in range(TT)]
        s_old = sem("s_old")
        const_made, consts_T, consts_ready, cond_ready = (sem(n) for n in
                                                          ("const_made", "consts_T", "consts_ready", "cond_ready"))
        first_used, mod_used, mod_evac = sem("first_used"), sem("mod_used"), sem("mod_evac")
        kq_hi, k_first = sem("kq_hi"), sem("k_first")
        modT_done, ab_ready = sem("modT_done"), sem("ab_ready")
        xsq_done, x_normed, x_new, xsq_l1 = (sem(n) for n in ("xsq_done", "x_normed", "x_new", "xsq_l1"))
        x_summed, x_rooted = sem("x_summed"), sem("x_rooted")
        h_tr, h_ev, h_ready = sem("h_tr"), sem("h_ev"), sem("h_ready")
        whi_ready, wlo_ready, mm_done, acc_done, acc_free = (sem(n) for n in
                                                             ("whi_ready", "wlo_ready", "mm_done", "acc_done", "acc_free"))
        ss_ready, roped, tr_done, tr_free, tab_ready = (sem(n) for n in
                                                        ("ss_ready", "roped", "tr_done", "tr_free", "tab_ready"))
        gate_ready = sem("gate_ready")
        sc_done, nm_ready, exp_done, pn_ready = (sem(n) for n in ("sc_done", "nm_ready", "exp_done", "pn_ready"))
        scx_done, pt_done, pt_act, pt_dve = (sem(n) for n in ("scx_done", "pt_done", "pt_act", "pt_dve"))
        o_done, gated, q_split, kv_main, kv_req = (sem(n) for n in ("o_done", "gated", "q_split", "kv_main", "kv_req"))
        dve_chain, act_chain, pool_chain = sem("dve_chain"), sem("act_chain"), sem("pool_chain")

        class Chain:

            def __init__(self, s):
                self.s, self.base, self.k, self.i, self.per = s, 0, 0, 0, 0

            def link(self, eng, ins):
                ins.then_inc(self.s, 1)
                self.k += 1
                eng.wait_ge(self.s, self.i * self.per + (self.base + self.k) if self.per else self.base + self.k)

            def enter(self, i, first, per):
                self.base += self.k - first * per
                self.k, self.i, self.per = 0, i, per

            def leave(self, end):
                assert self.k == self.per, (self.k, self.per)
                self.base += end * self.per
                self.k, self.per = 0, 0

        def w_col(ch):
            return {0: 4096, 1: 4608}.get(ch) if isinstance(ch, int) and ch < 2 else (ch - 2) * NC

        def key_parts(L, u):
            if u == TOK:
                return [(REQ, P)]
            if L == 1:
                return [(0, NC)]
            lo, hi = max(0, u - 1) * P, min(TOK, u + 2) * P
            return [(lo, CTX + P - lo)] if hi == CTX else [(lo, hi - lo), (CTX, P)]

        def key_tiles(L, u):
            if u == TOK:
                return [5]
            if L == 1:
                return [0, 1, 2, 3, 4]
            return list(range(max(0, u - 1), min(TOK, u + 2))) + [4]

        n_kt = [[len(key_tiles(L, u)) for u in range(TT)] for L in range(LAYERS)]
        n_even = [[(n + 1) // 2 for n in row] for row in n_kt]
        n_odd = [[n // 2 for n in row] for row in n_kt]

        def before(table, L, g, u):
            return sum(4 * sum(table[l]) for l in range(L)) + g * sum(table[L]) + sum(table[L][:u])

        def unit(L, g, u):
            return g * TT + (20 * L + u)

        def same_buffer(L, g, u):
            return unit(L, g, u) - (TT if u == TOK else 2 if u >= 2 else 3)

        Z_STORES = (3, 2)

        def buf(u):
            return 2 if u == TOK else u % 2

        def tr_number(L, X, t):
            return X * TT + (N_TR * L + t + (1 if not (isinstance(X, int) and X == 0) else 0))

        H0 = [0, 2 * KT]

        block = ctx.enter_context(nc.Block())

        @block.sync
        def _(sp):
            def mod_load(dst, L, kind, b, p, done):
                for kk in range(2):
                    rows = slice((2 * p + kk) * P, (2 * p + kk + 1) * P)
                    if kind == "S":
                        src = w_mod[L, rows, 0:2 * D].rearrange("p (s n) -> p s n", s=2)[:, :, ds(b * HALF, HALF)]
                        to = dst[:, kk, :].rearrange("p (s n) -> p s n", s=2)
                    else:
                        src, to = w_mod[L, rows, ds(b * MODB + 2 * D, MODB)], dst[:, kk, :]
                    sp.dma_start(to, src).then_inc(done, 16)

            def w_load(L, ch, src, n0, p):
                if not (isinstance(ch, int) and L == 0 and ch == 0 and p < 2):
                    sp.wait_ge(wlo_ready, (ch + 14 * L) * PAIRS + (p - 1))
                sp.dma_start(w_raw[:, p % 2], src[L, 2 * p * P:(2 * p + 2) * P, ds(n0, NC)]
                             .rearrange("(k p) n -> p k n", p=P)).then_inc(s_w[p % 2], 16)

            def chunk_loads(L, ch, src, n0, mod=None):
                for p in range(PAIRS):
                    w_load(L, ch, src, n0, p)
                    if mod is not None:
                        number, ml, kind, b = mod
                        if isinstance(number, int) and number == 0 and p < 2:
                            sp.wait_ge(first_used, GROUPS * PAIRS)
                        else:
                            sp.wait_ge(mod_used, number * PAIRS + (p - 1))
                        mod_load(mod_w[:, p % 2], ml, kind, b, p, s_mw[p % 2])

            for b in range(GROUPS):
                for p in range(PAIRS):
                    n = b * PAIRS + p
                    if n >= RING0:
                        sp.wait_ge(first_used, n - RING0 + 1)
                    mod_load(first_ring[n % RING0], 0, "S", b, p, s_first[n % RING0])
                if b == 0:
                    for t in range(TT):
                        src = x_sample[0, t * P:(t + 1) * P, :] if t < TOK else x_prompt[0]
                        sp.dma_start(x_tok[:, t, :], src).then_inc(s_x, 16)
                for p in (2 * b, 2 * b + 1):
                    w_load(0, 0, w_in, w_col(0), p)

            for L in range(LAYERS):
                if L == 1:
                    sp.wait_ge(x_new, TT * 4)
                    chunk_loads(L, 0, w_in, w_col(0), (6, 1, "G", 0))
                chunk_loads(L, 1, w_in, w_col(1), (0, 0, "G", 0) if L == 0 else (7, 1, "G", 1))
                chunk_loads(L, 2, w_in, 0, (1, 1, "S", 0) if L == 0 else None)
                with sp.Fori(1, 4) as i:
                    chunk_loads(L, i + 2, w_in, i * NC, (i + 1, 1, "S", i) if L == 0 else None)
                chunk_loads(L, FIRST_Z, w_in, D, (5, 0, "G", 1) if L == 0 else None)
                with sp.Fori(1, 4) as i:
                    chunk_loads(L, i + FIRST_Z, w_in, i * NC + D, None)
                chunk_loads(L, FIRST_O, w_out, 0, None)
                with sp.Fori(1, 4) as i:
                    chunk_loads(L, i + FIRST_O, w_out, i * NC, None)

        @block.gpsimd
        def _(pool):
            chain = Chain(pool_chain)
            g = nc.gpsimd
            g.memset(eps[:], EPS)
            g.memset(mod_ev[:], 0.0)
            for t in (ident, ident_b, mask_prev, mask_next):
                chain.link(pool, g.memset(t[:], 0.0))
            for t in (ident, ident_b):
                chain.link(pool, g.affine_select(out=t[:], in_=t[:], compare_op=ALU.not_equal, fill=1.0, base=0,
                                                 pattern=[[-1, P]], channel_multiplier=1))
            chain.link(pool, g.affine_select(out=mask_prev[:], in_=mask_prev[:], compare_op=ALU.is_ge, fill=NEG,
                                             base=0, pattern=[[1, P]], channel_multiplier=-1))
            g.affine_select(out=mask_next[:], in_=mask_next[:], compare_op=ALU.is_ge, fill=NEG, base=0,
                            pattern=[[-1, P]], channel_multiplier=1).then_inc(const_made, 1)
            pool.dma_start(rows[0:16, :], c.rearrange("a (j p) -> (a j) p", p=P)).then_inc(s_rows, 16)
            pool.dma_start(rows[16:32, :], c_ctx.rearrange("(j p) -> j p", p=P)).then_inc(s_rows, 16)
            pool.dma_start(rows[32:64, :], norm_g.rearrange("l (j p) -> (l j) p", p=P)).then_inc(s_rows, 16)
            for L in range(LAYERS):
                pool.dma_start(rows[64 + 32 * L:96 + 32 * L, :],
                               b_mod[L, 0:2 * D].rearrange("(j p) -> j p", p=P)).then_inc(s_rows, 16)
            pool.dma_start(sink[:, :], sinks[0:1, :].to_broadcast([P, HEADS])).then_inc(s_sink, 16)

            def gate_store(n, Q):
                pool.wait_ge(mod_evac, Q + 1)
                for r in range(2):
                    pool.dma_start(gate_rows[r:r + 1, n * MODB:(n + 1) * MODB].rearrange("r (j n) -> (r j) n", j=4),
                                   mod_ev[r:r + 97:32, :]).then_inc(s_gate, 16)

            def table_loads(n, norm):
                if n > 0:
                    pool.wait_ge(roped, 5 if n == 1 else 25 if n == 2 else 30)
                pool.dma_start(rope_c[:, :, :], rope_cos.rearrange("(t p) d -> p t d", p=P)).then_inc(s_tab, 16)
                pool.dma_start(rope_s[:, :, :], rope_sin.rearrange("(t p) d -> p t d", p=P)).then_inc(s_tab, 16)
                pool.dma_start(gain[:, :], norm.to_broadcast([P, P])).then_inc(s_tab, 16)

            def z_stores(L, X):
                for t in range(TT):
                    pool.wait_ge(tr_free, tr_number(L, X, t) + 1)
                    pool.dma_start(z_spill[ds(X - 5, 1), t].rearrange("g p n -> (g p) n"),
                                   (t1, t2)[t % 2][:, :]).then_inc(s_zout[t % 2], 16)

            table_loads(0, k_norm_g[0:1, :])
            for L in range(LAYERS):
                if L == 1:
                    gate_store(2, 10)
                pool.wait_ge(roped, 25 * L + TT)
                pool.dma_start(new_k[0, L].rearrange("p h d -> p (h d)"), stage[:, TOK, :]).then_inc(s_newk, 16)
                pool.dma_start(v_tok[:, 4, :], cache_v[0, L].rearrange("p h d -> p (h d)")).then_inc(s_cv, 16)
                gate_store(*((0, 4) if L == 0 else (3, 11)))
                pool.wait_ge(tr_done, tr_number(L, 0, 4) + 1)
                pool.dma_start(stage[:, 0, :], cache_k[0, L].rearrange("p h d -> p (h d)")).then_inc(s_ck, 16)
                table_loads(2 * L + 1, q_norm_g[L:L + 1, :])
                pool.wait_ge(acc_free, (14 * L + 2) * TT)
                pool.dma_start(new_v[0, L].rearrange("p h d -> p (h d)"), v_tok[:, 5, :]).then_inc(s_newv, 16)
                if L == 0:
                    table_loads(2, k_norm_g[1:2, :])
                    gate_store(1, 9)
                for X in (5, 6, 7):
                    z_stores(L, X)

                def k_split(gg, first, n, prev, done):
                    pool.wait_ge(sc_done, prev * 4 + (4 * CREDIT + 4))
                    src = kT[:, ds(gg, 1), first:first + n].rearrange("p g k -> p (g k)")
                    g.tensor_copy(k_hi[:, first:first + n], src)
                    pool.drain()
                    g.tensor_tensor(k_lo[:, first:first + n], src, k_hi[:, first:first + n].bitcast(f32),
                                    ALU.subtract).then_inc(done, 1)

                def v_copy(gg, first, n, prev, done):
                    pool.wait_ge(o_done, prev + (CREDIT + 1))
                    g.tensor_copy(v_g[:, first // P:(first + n) // P, :],
                                  v_tok[:, first // P:(first + n) // P, ds(gg * P, P)]).then_inc(done, 1)

                def q_split_unit(gg, u):
                    U, prev = unit(L, gg, u), same_buffer(L, gg, u)
                    pool.wait_ge(sc_done, prev * 4 + (4 * CREDIT + 4))
                    src = qT[:, ds(gg, 1), u, :].rearrange("p g n -> p (g n)")
                    g.tensor_copy(q_hi[buf(u)][:, :], src)
                    pool.drain()
                    g.tensor_tensor(q_lo[buf(u)][:, :], src, q_hi[buf(u)][:, :].bitcast(f32), ALU.subtract).then_inc(q_split, 1)

                def z_load(gg, u):
                    pool.wait_ge(gated, unit(L, gg, u) + (CREDIT - TT + 1))
                    pool.dma_start(z_in[:, u, :], z_spill[ds(gg, 1), u].rearrange("g p n -> (g p) n")
                                   ).then_inc(s_zin[u], 16)

                pool.wait_ge(acc_done, (14 * L + FIRST_O) * TT)
                pool.wait_ge(tr_free, tr_number(L, 4, 4) + 1)
                pool.wait_ge(s_cv, 16 * (L + 1))
                v_copy(0, 0, 5 * P, unit(L, 0, 0) - 2, kv_main)
                z_stores(L, 8)
                for i in range(2):
                    pool.wait_ge(s_zout[i], 64 * Z_STORES[i] * (L + 1))

                def pool_group(gg, last):
                    for u in range(TT):
                        z_load(gg, u)
                        if u < TOK:
                            q_split_unit(gg, u + 1)
                        elif not last:
                            k_split(gg + 1, 0, 5 * P, unit(L, gg, 3), kv_main)
                            q_split_unit(gg + 1, 0)
                            v_copy(gg + 1, 0, 5 * P, unit(L, gg, 3), kv_main)
                        if u == 0:
                            k_split(gg, REQ, P, unit(L, gg, 0) - 1, kv_req)
                            v_copy(gg, REQ, P, unit(L, gg, 0) - 1, kv_req)

                with pool.Fori(0, 3) as gg:
                    pool_group(gg, False)
                pool_group(3, True)

                def out_loads(n):
                    if isinstance(n, int) and n == 0:
                        pool.wait_ge(mod_used, PAIRS * (6 if L == 0 else 8))
                        pool.wait_ge(s_gate, 64 * (L + 1))
                        if L == 1:
                            pool.wait_ge(s_y, 16 * TT * 3)
                            pool.wait_ge(s_y3, 16 * TT)
                    else:
                        pool.wait_ge(x_new, n * TT + 20 * L)
                    for t in range(TT):
                        if L == 1:
                            src = x_spill[t, :, ds(n * NC, NC)]
                        elif t < TOK:
                            src = x_sample[0, t * P:(t + 1) * P, ds(n * NC, NC)]
                        else:
                            src = x_prompt[0, :, ds(n * NC, NC)]
                        pool.dma_start(x_old[:, t, :], src).then_inc(s_old, 16)
                    col = n * NC + D * L
                    for r in range(2):
                        pool.dma_start(gate[:, r, :], gate_rows[r:r + 1, ds(col, NC)].to_broadcast([P, NC])
                                       ).then_inc(s_old, 16)
                    pool.dma_start(gate_b, b_mod[L:L + 1, ds(n * NC + 2 * D, NC)].to_broadcast([P, NC])
                                   ).then_inc(s_old, 16)

                def out_stores(n, done):
                    for t in range(TT):
                        pool.wait_ge(x_new, n * TT + (20 * L + t + 1))
                        if L == 0:
                            dst = x_spill[t, :, ds(n * NC, NC)]
                        elif t < TOK:
                            dst = y_sample[0, t * P:(t + 1) * P, ds(n * NC, NC)]
                        else:
                            dst = y_prompt[0, :, ds(n * NC, NC)]
                        pool.dma_start(dst, x_tok[:, t, ds(n * NC, NC)]).then_inc(done, 16)

                out_loads(0)
                out_stores(0, s_y)
                with pool.Fori(1, 3) as n:
                    out_loads(n)
                    out_stores(n, s_y)
                out_loads(3)
                out_stores(3, s_y3)

            pool.wait_ge(s_newk, 16 * LAYERS)
            pool.wait_ge(s_newv, 16 * LAYERS)
            pool.wait_ge(s_y, 16 * TT * 3 * LAYERS)
            pool.wait_ge(s_y3, 16 * TT * LAYERS)
            pool.wait_ge(s_gate, 64 * LAYERS)
            for i in range(2):
                pool.wait_ge(s_zout[i], 64 * Z_STORES[i] * LAYERS)

        @block.scalar
        def _(act):
            chain = Chain(act_chain)
            s = nc.scalar
            act.wait_ge(consts_ready, 1)
            s.activation(cond[:, :, :].rearrange("p k r -> p r k"), consts[:, 0:32].rearrange("p (r k) -> p r k", r=2),
                         ACT.Silu).then_inc(cond_ready, 1)

            def first_squares():
                act.wait_ge(s_x, 16 * TT)
                for n in range(4):
                    for t in range(TT):
                        ins = s.activation(stage[:, t, :], x_tok[:, t, n * NC:(n + 1) * NC], ACT.Square,
                                           accum_out=ss_x[:, t, n:n + 1])
                        if t == TT - 1 and n < 3:
                            chain.link(act, ins)
                        elif t == TT - 1:
                            ins.then_inc(xsq_done, 1)

            def mod_evacuate(used, count, transposed=None, stored=None):
                act.wait_ge(used, count)
                if transposed is not None:
                    act.wait_ge(modT_done, transposed)
                if stored is not None:
                    act.wait_ge(s_gate, stored)
                for j in range(4):
                    ins = s.copy(mod_ev[32 * j:32 * j + 2, :], bank[MODBANK][32 * j:32 * j + 2, 0:256])
                ins.then_inc(mod_evac, 1)

            def split_hi(L, ch, p):
                C = ch + 14 * L
                act.wait_ge(s_w[p % 2], C * 64 + 16 * (p // 2 + 1))
                start = isinstance(ch, int) and L == 0 and ch == 0
                if p == 0 and not start:
                    act.wait_ge(mm_done, C * 7)
                elif p == 1 and not start:
                    act.wait_ge(acc_done, C * TT)
                elif p >= 2:
                    act.wait_ge(mm_done, C * 7 + (p - 1))
                s.copy(w_hi[:, p % 2], w_raw[:, p % 2]).then_inc(whi_ready, 1)

            def evacuate(L, ch, kind, X):
                C = ch + 14 * L
                for t in range(TT):
                    act.wait_ge(acc_done, C * TT + (t - 4))
                    if kind == "v":
                        s.copy(v_tok[:, t if t < TOK else 5, :], bank[t][:, :]).then_inc(acc_free, 1)
                        continue
                    if kind == "k":
                        act.wait_ge(h_ready, H0[L] + KT)
                    else:
                        act.wait_ge(tr_done, X * TT + (N_TR * L + t - TT + 2))
                    s.activation(stage[:, t, :], bank[t][:, :], ACT.Silu if kind == "z" else ACT.Copy
                                 ).then_inc(acc_free, 1)

            def head_squares(L, X):
                R = X * TT + 25 * L
                if not (isinstance(X, int) and X == 0 and L == 0):
                    act.wait_ge(roped, R)
                act.wait_ge(acc_free, (14 * L + 1 + X + (0 if isinstance(X, int) and X == 0 else 1)) * TT)
                for t in range(TT):
                    for h in range(4):
                        chain.link(act, s.activation(junk[:, :], stage[:, t, h * P:(h + 1) * P], ACT.Square,
                                                     accum_out=ss_h[:, t, h:h + 1]))
                    s.activation(rms_h[:, t, :], ss_h[:, t, :], ACT.Sqrt, bias=eps[:, :], scale=1.0 / P
                                 ).then_inc(ss_ready, 1)

            def evac_transposed(L, kind, X, t):
                n = tr_number(L, X, t)
                act.wait_ge(tr_done, n + 1)
                src = bank[6 + t % 2]
                if kind == "k":
                    col = t * P if t < TOK else REQ
                    dst, src = kT[:, :, col:col + P], src[:, :].rearrange("p (g n) -> p g n", g=4)
                elif kind == "q":
                    dst, src = qT[:, ds(X - 1, 1), t, :].rearrange("p g n -> p (g n)"), src[:, :]
                else:
                    if isinstance(X, int) and X == 5 and t < 2:
                        act.wait_ge(roped, 25 * (L + 1))
                    if not (isinstance(X, int) and X == 5 and t < 2 and L == 0):
                        act.wait_ge(s_zout[t % 2], (X - 5) * (16 * Z_STORES[t % 2]) + (64 * Z_STORES[t % 2] * L + 16 * (t // 2)))
                    dst, src = (t1, t2)[t % 2][:, :], src[:, :]
                s.copy(dst, src).then_inc(tr_free, 1)

            def h_evacuate(L, kt):
                act.wait_ge(h_tr, KT * L + kt + 1)
                if kt >= 2:
                    act.wait_ge(h_ready, H0[L] + kt - 1)
                elif kt == 0:
                    act.wait_ge(ab_ready, L + 1)
                    act.wait_ge(*((xsq_done, 1) if L == 0 else (xsq_l1, 20 + TT)))
                s.activation(h32[:, kt % 2, 0:NC], bank[6][:, :], ACT.Identity,
                             bias=addB[:, kt, 0:1], scale=mulA[:, kt, 0:1])
                s.activation(h32[:, kt % 2, NC:NC + P], bank[7][:, 0:P], ACT.Identity,
                             bias=addB[:, kt, 1:2], scale=mulA[:, kt, 1:2]).then_inc(h_ev, 1)

            def gated_hi(L, kt):
                src = qT[:, kt // 4, :, (kt % 4) * P:(kt % 4 + 1) * P]
                s.copy(hT_hi[:, kt, :].rearrange("p (t n) -> p t n", t=TT), src).then_inc(h_ev, 1)

            def chunk(L, ch, kind, X, mod=None):
                split_hi(L, ch, 0)
                if kind in ("k", "v", "q", "z"):
                    evacuate(L, ch, kind, X)
                split_hi(L, ch, 1)
                if mod is not None:
                    mod_evacuate(mod_used, *mod)
                if kind in ("k", "q"):
                    head_squares(L, X)
                for p in range(2, PAIRS):
                    split_hi(L, ch, p)
                    if kind in ("k", "q", "z") and p - 2 < TT:
                        evac_transposed(L, kind, X, p - 2)
                    if kind == "v" and p == 3:
                        act.wait_ge(tr_done, N_TR * L + TT + 1)
                        s.copy(kT[:, :, CTX:CTX + P], bank[7][:, :].rearrange("p (g n) -> p g n", g=4)
                               ).then_inc(tr_free, 1)
                    if kind == "o" and L == 0 and p - 2 < TT:
                        new_square(ch - FIRST_O - 1, p - 2)
            def new_square(n, t):
                act.wait_ge(x_new, n * TT + (t + 1))
                s.activation(stage[:, t, :], x_tok[:, t, ds(n * NC, NC)], ACT.Square,
                             accum_out=ss_x[:, t, ds(n, 1)]).then_inc(xsq_l1, 1)

            for L in range(LAYERS):
                def x_root():
                    act.wait_ge(x_summed, L + 1)
                    s.activation(rms_x[:, :], sum_x[:, :], ACT.Sqrt, bias=eps[:, :], scale=1.0 / D).then_inc(x_rooted, 1)

                if L == 0:
                    act.wait_ge(const_made, 1)
                    for b in range(GROUPS):
                        mod_evacuate(first_used, (b + 1) * PAIRS, transposed=b or None)
                        if b == 0:
                            first_squares()
                            x_root()
                        split_hi(0, 0, 2 * b)
                        split_hi(0, 0, 2 * b + 1)
                        for kt in range(PER * b, PER * b + PER):
                            h_evacuate(0, kt)
                else:
                    split_hi(L, 0, 0)
                    x_root()
                    for p in range(PAIRS):
                        if p:
                            split_hi(L, 0, p)
                        for kt in (2 * p, 2 * p + 1):
                            h_evacuate(L, kt)
                chunk(L, 1, "k", 0, None if L == 0 else (7 * PAIRS, 8, 64))
                chunk(L, 2, "v", None, (PAIRS, 4, None) if L == 0 else (8 * PAIRS, None, 96))
                act.wait_ge(s_newk, 16 * (L + 1))
                with act.Fori(1, 4) as i:
                    chain.enter(i, 1, 4 * TT)
                    chunk(L, i + 2, "q", i, (i * PAIRS + PAIRS, i + 3, 32) if L == 0 else None)
                    chain.leave(4)
                chunk(L, FIRST_Z, "q", 4, (5 * PAIRS, 7, 32) if L == 0 else None)
                if L == 0:
                    mod_evacuate(mod_used, 6 * PAIRS, 8)
                with act.Fori(1, 4) as i:
                    chunk(L, i + FIRST_Z, "z", i + 4)
                act.wait_ge(acc_done, (14 * L + FIRST_O) * TT)
                act.wait_ge(tr_free, tr_number(L, 4, 4) + 1)
                s.copy(k_hi[:, 0:5 * P], kT[:, 0, 0:5 * P])
                s.copy(q_hi[0][:, :], qT[:, 0, 0, :]).then_inc(kq_hi, 1)
                evacuate(L, FIRST_O, "z", 8)
                for t in range(TT):
                    evac_transposed(L, "z", 8, t)

                def exps(gg, u, h):
                    U, prev = unit(L, gg, u), same_buffer(L, gg, u)
                    b, n = buf(u), P * n_kt[L][u]
                    if h % 2 == 0:
                        act.wait_ge(nm_ready, U * 2 + (h // 2 + 1))
                    if h == 0:
                        act.wait_ge(o_done, prev + (CREDIT + 1))
                    m = min(n, NC)
                    ins = s.activation(probs[b][:, h, 0:m], bank[h][:, 0:m], ACT.Exp, bias=nmax[:, h:h + 1],
                                       scale=SCALE, accum_out=den[:, h:h + 1])
                    if n > NC:
                        ins = s.activation(probs[b][:, h, NC:n], bank[4][:, h * P:(h + 1) * P], ACT.Exp,
                                           bias=nmax[:, h:h + 1], scale=SCALE, accum_out=denx[:, h:h + 1])
                    if L == 0 and h == 3:
                        ins = s.activation(denx[:, :], sinkd[:, :], ACT.Exp)
                    ins.then_inc(exp_done, 1)

                def probs_out(gg, u, kt):
                    U, prev = unit(L, gg, u), same_buffer(L, gg, u)
                    act.wait_ge(pt_done, before(n_kt, L, gg, u) + (kt + 1))
                    if kt == 0:
                        act.wait_ge(o_done, prev + (CREDIT + 1))
                    s.copy(probsT[buf(u)][:, kt, :], bank[5 + kt % 2][:, :]).then_inc(pt_act, 1)

                def act_group(gg, last):
                    for u in range(TT):
                        even = list(range(0, n_kt[L][u], 2))
                        for kt in even[:2]:
                            probs_out(gg, u, kt)
                        for h in range(4):
                            if not (last and u == TOK):
                                exps(*((gg, u + 1) if u < TOK else (gg + 1, 0)), h)
                            if h == 1:
                                for kt in even[2:]:
                                    probs_out(gg, u, kt)

                for h in range(4):
                    exps(0, 0, h)
                with act.Fori(0, 3) as gg:
                    act_group(gg, False)
                act_group(3, True)

                if L == 0:
                    chain.link(act, s.activation(junk[:, 0:1], eps[:, :], ACT.Sqrt))
                split_hi(L, FIRST_O, 0)
                for p in range(PAIRS):
                    if p:
                        split_hi(L, FIRST_O, p)
                    for kt in (2 * p, 2 * p + 1):
                        if kt == 0:
                            act.wait_ge(gated, CREDIT + 20 * (L + 1))
                            act.wait_ge(o_done, CREDIT + 20 * (L + 1))
                        gated_hi(L, kt)
                with act.Fori(1, 4) as n:
                    chunk(L, n + FIRST_O, "o", None)
                if L == 0:
                    for t in range(TT):
                        new_square(3, t)

        @block.vector
        def _(dve):
            chain = Chain(dve_chain)
            v = nc.vector
            dve.wait_ge(s_sink, 16)
            chain.link(dve, v.tensor_scalar(neg_sink[:, :], sink[:, :], -1.0, None, ALU.mult))
            dve.wait_ge(consts_T, 1)
            v.tensor_copy(consts[:, :], bank[7][:, 0:P]).then_inc(consts_ready, 1)

            def x_norm(L):
                if L == 0:
                    dve.wait_ge(xsq_done, 1)
                    dve.wait_ge(s_x, 16 * TT)
                else:
                    dve.wait_ge(xsq_l1, 20 + TT)
                v.tensor_reduce(sum_x[:, :], ss_x[:, :, :], AX, ALU.add).then_inc(x_summed, 1)
                dve.wait_ge(x_rooted, L + 1)
                chain.link(dve, v.reciprocal(r_x[:, :], rms_x[:, :]))
                for n in range(4):
                    if L == 1 and n == 0:
                        dve.wait_ge(s_y, 16 * TT * 3)
                    if L == 1 and n == 3:
                        dve.wait_ge(s_y3, 16 * TT)
                    for t in range(TT):
                        ins = v.tensor_scalar(x_tok[:, t, n * NC:(n + 1) * NC], x_tok[:, t, n * NC:(n + 1) * NC],
                                              r_x[:, t:t + 1], None, ALU.mult)
                    ins.then_inc(x_normed, 1)

            def scale_shift(L, b):
                dve.wait_ge(modT_done, b + (GROUPS * L + 1))
                src = bank[7][:, 0:256].rearrange("p (s j r) -> p j s r", s=2, j=4)
                at = b * PER

                def both(a):
                    return a.rearrange("p (j s r) -> p j s r", s=2, r=1).to_broadcast([P, 2, 2, 2])

                def part(t):
                    return t[:, ds(at, PER), :].rearrange("p (j s) r -> p j s r", s=2)

                v.tensor_tensor(part(addB), src[:, 0:2, :, 0:2], both(consts[:, ds(at + (64 + 32 * L), PER)]), ALU.add)
                chain.link(dve, v.tensor_tensor(part(mulA), src[:, 2:4, :, 0:2],
                                                both(consts[:, ds(at + (64 + 32 * L + KT), PER)]), ALU.add))
                v.scalar_tensor_tensor(part(mulA), part(mulA), 1.0, both(consts[:, ds(at + (32 + 16 * L), PER)]),
                                       ALU.add, ALU.mult).then_inc(ab_ready, 1)

            def tables(n):
                dve.wait_ge(s_tab, 48 * (n + 1))
                gb = gain[:, :].rearrange("p (t d) -> p t d", t=1).to_broadcast([P, TOK, P])
                chain.link(dve, v.tensor_tensor(rope_c[:, :, :], rope_c[:, :, :], gb, ALU.mult))
                for a in range(2):
                    for hf in range(2):
                        o, other = 64 * a + 32 * hf, 64 * a + 32 * (1 - hf)
                        gs = gain[:, other:other + 32].rearrange("p (t d) -> p t d", t=1).to_broadcast([P, TOK, 32])
                        ins = v.tensor_tensor(rope_s[:, :, o:o + 32], rope_s[:, :, o:o + 32], gs, ALU.mult)
                chain.link(dve, ins)

            def split_lo(L, ch, p):
                C = ch + 14 * L
                dve.wait_ge(whi_ready, C * PAIRS + (p + 1))
                dve.wait_ge(s_w[p % 2], C * 64 + 16 * (p // 2 + 1))
                v.tensor_tensor(w_lo[:, p % 2], w_raw[:, p % 2], w_hi[:, p % 2].bitcast(f32),
                                ALU.subtract).then_inc(wlo_ready, 1)

            def norm_rope(L, X, t):
                R = X * TT + (25 * L + t)
                dve.wait_ge(ss_ready, R + 1)
                chain.link(dve, v.reciprocal(r_h[:, :], rms_h[:, t, :]))
                st = stage[:, t, :].rearrange("p (h d) -> p h d", h=4)
                rb = r_h[:, :].rearrange("p (h d) -> p h d", d=1).to_broadcast([P, 4, P])
                chain.link(dve, v.tensor_tensor(st, st, rb, ALU.mult))
                if t == TOK:
                    gb = gain[:, :].rearrange("p (h d) -> p h d", h=1).to_broadcast([P, 4, P])
                    v.tensor_tensor(st, st, gb, ALU.mult).then_inc(roped, 1)
                    dve.wait_ge(roped, R + 1)
                    return
                a1 = t1[:, :].rearrange("p (h d) -> p h d", h=4)
                a2 = t2[:, :].rearrange("p (ha f d) -> p ha f d", f=2, d=32)
                sf = stage[:, t, :].rearrange("p (ha f d) -> p ha f d", f=2, d=32)
                cb = rope_c[:, t:t + 1, :].to_broadcast([P, 4, P])
                v.tensor_tensor(a1, st, cb, ALU.mult)
                for hf in range(2):
                    for a in range(2):
                        o = 64 * a + 32 * hf
                        x_other = stage[:, t, :].rearrange("p (h d) -> p h d", h=4)[:, :, 64 * a + 32 * (1 - hf):64 * a + 32 * (1 - hf) + 32]
                        dst = t2[:, :].rearrange("p (h d) -> p h d", h=4)[:, :, o:o + 32]
                        ins = v.tensor_tensor(dst, x_other, rope_s[:, t:t + 1, o:o + 32].to_broadcast([P, 4, 32]), ALU.mult)
                chain.link(dve, ins)
                v.tensor_tensor(stage[:, t, :], t1[:, :], t2[:, :], ALU.add).then_inc(roped, 1)
                dve.wait_ge(roped, R + 1)

            LINKS_Q = 2 * TT + TOK

            def gate_add(L, n):
                dve.wait_ge(s_old, (n * 128 + 128 * (4 * L + 1)) if not isinstance(n, int) else 128 * (4 * L + n + 1))
                for_both = gate_b.rearrange("p (r n) -> p r n", r=1).to_broadcast([P, 2, NC])
                chain.link(dve, v.tensor_tensor(gate, gate, for_both, ALU.add))

            def gate_out(L, n, t):
                dve.wait_ge(acc_done, n * TT + (TT * (14 * L + FIRST_O) + t + 1))
                if L == 0:
                    dve.wait_ge(xsq_l1, n * TT + (t + 1))
                v.tensor_tensor(stage[:, t, :], bank[t][:, :], gate[:, 0 if t < TOK else 1, :],
                                ALU.mult).then_inc(acc_free, 1)

            def add_x(L, n, t):
                dve.wait_ge(acc_free, n * TT + (TT * (14 * L + FIRST_O) + t + 1))
                v.tensor_tensor(x_tok[:, t, ds(n * NC, NC)], stage[:, t, :], x_old[:, t, :],
                                ALU.add).then_inc(x_new, 1)

            def chunk(L, ch, kind, X, mod=None):
                split_lo(L, ch, 0)
                if kind == "o":
                    gate_add(L, ch - FIRST_O - 1)
                    for t in range(TT):
                        gate_out(L, ch - FIRST_O - 1, t)
                split_lo(L, ch, 1)
                if mod is not None:
                    scale_shift(1, mod)
                for p in range(2, PAIRS):
                    if p - 2 < TT:
                        if kind in ("k", "q"):
                            norm_rope(L, X, p - 2)
                        if kind == "o":
                            add_x(L, ch - FIRST_O - 1, p - 2)
                    split_lo(L, ch, p)

            tables(0)
            for L in range(LAYERS):
                def h_split(kt):
                    dve.wait_ge(h_ev, H0[L] + kt + 1)
                    chain.link(dve, v.tensor_copy(hT_hi[:, kt, :], h32[:, kt % 2, :]))
                    v.tensor_tensor(hT_lo[:, kt, :], h32[:, kt % 2, :], hT_hi[:, kt, :].bitcast(f32),
                                    ALU.subtract).then_inc(h_ready, 1)

                if L == 0:
                    dve.wait_ge(consts_ready, 1)
                    for b in range(GROUPS):
                        scale_shift(0, b)
                        if b == 0:
                            x_norm(0)
                        if b == GROUPS - 1:
                            dve.wait_ge(first_used, GROUPS * PAIRS)
                        split_lo(0, 0, 2 * b)
                        split_lo(0, 0, 2 * b + 1)
                        for kt in range(PER * b, PER * b + PER):
                            h_split(kt)
                else:
                    split_lo(L, 0, 0)
                    x_norm(1)
                    dve.wait_ge(acc_done, 14 * TT)
                    for p in range(PAIRS):
                        if p:
                            split_lo(L, 0, p)
                        for kt in (2 * p, 2 * p + 1):
                            h_split(kt)
                chunk(L, 1, "k", 0)
                split_lo(L, 2, 0)
                split_lo(L, 2, 1)
                tables(2 * L + 1)
                for p in range(2, PAIRS):
                    split_lo(L, 2, p)
                with dve.Fori(1, 4) as i:
                    chain.enter(i, 1, LINKS_Q + (1 if L == 0 else 0))
                    chunk(L, i + 2, "q", i, i - 1 if L == 0 else None)
                    chain.leave(4)
                chunk(L, FIRST_Z, "q", 4, 3 if L == 0 else None)
                with dve.Fori(1, 4) as i:
                    chunk(L, i + FIRST_Z, None, None)
                if L == 0:
                    tables(2)

                def ctx_maxima(gg, u):
                    dve.wait_ge(scx_done, gg * TOK + (u + 1))
                    v.tensor_reduce(mxc[:, :], bank[4][:, :].rearrange("p (h k) -> p h k", h=4), AX, ALU.max)

                def maxima(gg, u, h0):
                    U, n, hs = unit(L, gg, u), P * n_kt[L][u], slice(h0, h0 + 2)
                    for h in (h0, h0 + 1):
                        dve.wait_ge(sc_done, U * 4 + (4 * CREDIT + h + 1))
                        ins = v.tensor_reduce(mx[:, h:h + 1], bank[h][:, 0:min(n, NC)], AX, ALU.max)
                    chain.link(dve, ins)
                    if n > NC:
                        chain.link(dve, v.tensor_tensor(mx[:, hs], mx[:, hs], mxc[:, hs], ALU.max))
                    if L == 1:
                        v.tensor_scalar(nmax[:, hs], mx[:, hs], -SCALE, None, ALU.mult).then_inc(nm_ready, 1)
                    else:
                        chain.link(dve, v.scalar_tensor_tensor(nmax[:, hs], mx[:, hs], -SCALE,
                                                               neg_sink[:, ds(gg * 4 + h0, 2)], ALU.mult, ALU.min))
                        v.tensor_tensor(sinkd[:, hs], nmax[:, hs], sink[:, ds(gg * 4 + h0, 2)], ALU.add
                                        ).then_inc(nm_ready, 1)

                def normalise(gg, u):
                    U, b, n = unit(L, gg, u), buf(u), P * n_kt[L][u]
                    dve.wait_ge(exp_done, U * 4 + 8)
                    if L == 0 or n > NC:
                        chain.link(dve, v.tensor_tensor(rden[:, :], den[:, :], denx[:, :], ALU.add))
                        chain.link(dve, v.reciprocal(rden[:, :], rden[:, :]))
                    else:
                        chain.link(dve, v.reciprocal(rden[:, :], den[:, :]))
                    for h in range(4):
                        ins = v.tensor_scalar(probs[b][:, h, 0:n], probs[b][:, h, 0:n], rden[:, h:h + 1], None, ALU.mult)
                    ins.then_inc(pn_ready, 1)

                def probs_out(gg, u, kt):
                    U, prev = unit(L, gg, u), same_buffer(L, gg, u)
                    dve.wait_ge(pt_done, before(n_kt, L, gg, u) + (kt + 1))
                    if kt == 1:
                        dve.wait_ge(o_done, prev + (CREDIT + 1))
                    v.tensor_copy(probsT[buf(u)][:, kt, :], bank[5 + kt % 2][:, :]).then_inc(pt_dve, 1)

                def gate_unit(gg, u):
                    U = unit(L, gg, u)
                    dve.wait_ge(o_done, U + (CREDIT + 1))
                    dve.wait_ge(s_zin[u], gg * 16 + 16 * (4 * L + 1))
                    if not (isinstance(gg, int) and gg == 0 and u == 0):
                        dve.wait_ge(q_split, U - L)
                    dst = qT[:, ds(gg, 1), u, :].rearrange("p g n -> p (g n)")
                    v.tensor_tensor(dst, bank[7][:, :], z_in[:, u, :], ALU.mult).then_inc(gated, 1)

                def dve_group(gg, last):
                    for u in range(TT):
                        ng, nu = (gg, u + 1) if u < TOK else (gg + 1, 0)
                        more = not (last and u == TOK)
                        odd = list(range(1, n_kt[L][u], 2))
                        if more and L == 1 and nu < TOK:
                            ctx_maxima(ng, nu)
                        for h0 in (0, 2):
                            if more:
                                maxima(ng, nu, h0)
                            if odd:
                                probs_out(gg, u, odd.pop(0))
                        if more:
                            normalise(ng, nu)
                        gate_unit(gg, u)

                dve.wait_ge(kq_hi, L + 1)
                v.tensor_tensor(k_lo[:, 0:5 * P], kT[:, 0, 0:5 * P], k_hi[:, 0:5 * P].bitcast(f32),
                                ALU.subtract).then_inc(k_first, 1)
                v.tensor_tensor(q_lo[0][:, :], qT[:, 0, 0, :], q_hi[0][:, :].bitcast(f32), ALU.subtract).then_inc(k_first, 1)
                if L == 1:
                    ctx_maxima(0, 0)
                for h0 in (0, 2):
                    maxima(0, 0, h0)
                normalise(0, 0)
                m0, m1 = (4, 4) if L == 0 else (4, 2)
                n0, n1 = (2, 2) if L == 0 else (2, 1)
                per = TOK * (m0 + n0) + m1 + n1
                with dve.Fori(0, 3) as gg:
                    chain.enter(gg, 0, per)
                    dve_group(gg, False)
                    chain.leave(3)
                dve_group(3, True)

                split_lo(L, FIRST_O, 0)
                for p in range(PAIRS):
                    if p:
                        split_lo(L, FIRST_O, p)
                    for kt in (2 * p, 2 * p + 1):
                        dve.wait_ge(h_ev, H0[L] + KT + kt + 1)
                        src = qT[:, kt // 4, :, (kt % 4) * P:(kt % 4 + 1) * P]
                        v.tensor_tensor(hT_lo[:, kt, :].rearrange("p (t n) -> p t n", t=TT), src,
                                        hT_hi[:, kt, :].bitcast(f32).rearrange("p (t n) -> p t n", t=TT),
                                        ALU.subtract).then_inc(h_ready, 1)
                dve.wait_ge(h_ready, H0[L] + 2 * KT)
                with dve.Fori(1, 4) as n:
                    chain.enter(n, 1, 1)
                    chunk(L, n + FIRST_O, "o", None)
                    chain.leave(4)
                gate_add(L, 3)
                for t in range(TT):
                    gate_out(L, 3, t)
                for t in range(TT):
                    add_x(L, 3, t)
        @block.tensor
        def _(pe):
            mm = nc.tensor.matmul
            pe.sem_inc(o_done, CREDIT)
            pe.sem_inc(gated, CREDIT)
            pe.sem_inc(sc_done, 4 * CREDIT)
            pe.sem_inc(exp_done, 4)
            pe.sem_inc(xsq_l1, TT)
            pe.sem_inc(pt_act, 1)
            pe.sem_inc(pt_dve, 1)
            pe.wait_ge(const_made, 1)
            pe.wait_ge(s_rows, 80)
            nc.tensor.transpose(bank[7][:, 0:P], rows[:, :], ident[:, :]).then_inc(consts_T, 1)
            pe.wait_ge(cond_ready, 1)

            def mod_products(w, s, used):
                for kk in range(2):
                    k = 2 * s + kk
                    for j in range(4):
                        ins = mm(bank[MODBANK][32 * j:32 * j + 2, 0:256], cond[:, k, :], w[:, kk, j * 256:(j + 1) * 256],
                                 start=(k == 0), stop=(k == KT - 1))
                ins.then_inc(used, 1)

            def first_item(b, s):
                n = b * PAIRS + s
                if s == 0 and b > 0:
                    pe.wait_ge(mod_evac, b)
                pe.wait_ge(s_first[n % RING0], 32 * (n // RING0 + 1))
                mod_products(first_ring[n % RING0], s, first_used)

            def mod_transpose(n, Q):
                pe.wait_ge(mod_evac, Q + 1)
                for h in range(2):
                    ins = nc.tensor.transpose(bank[7][:, h * P:(h + 1) * P], mod_ev[:, h * P:(h + 1) * P], ident[:, :])
                ins.then_inc(modT_done, 1)

            def chunk(L, ch, kind, X, mod=None, fresh=None, rows=None):
                C = ch + 14 * L
                start = isinstance(ch, int) and ch == 0 and L == 0
                for p in range(PAIRS):
                    for kk in range(2):
                        k = 2 * p + kk
                        if fresh == "x" and L == 0:
                            if k % PER == 0:
                                pe.wait_ge(h_ev, k) if k else pe.wait_ge(consts_ready, 1)
                                mod_transpose(k // PER, k // PER)
                                h_transposes(L, k)
                            if k % PER < PER - 1:
                                h_transposes(L, k + 1)
                        elif fresh == "x":
                            for kt in ((0, 1, 2) if k == 0 else (k + 2,)):
                                if kt < KT:
                                    h_transposes(L, kt)
                        if kk == 0:
                            pe.wait_ge(wlo_ready, C * PAIRS + (p + 1))
                        if fresh is not None:
                            pe.wait_ge(h_ready, H0[L] + (KT if fresh == "o" else 0) + k + 1)
                        for t in range(TT):
                            if k == 0 and not start:
                                pe.wait_ge(acc_free, C * TT + (t - 4))
                            hi, lo = hT_hi[:, k, t * P:(t + 1) * P], hT_lo[:, k, t * P:(t + 1) * P]
                            mm(bank[t][:, :], hi, w_hi[:, p % 2, kk], start=(k == 0), stop=False)
                            mm(bank[t][:, :], hi, w_lo[:, p % 2, kk], start=False, stop=False)
                            ins = mm(bank[t][:, :], lo, w_hi[:, p % 2, kk], start=False, stop=(k == KT - 1))
                            if k == KT - 1:
                                ins.then_inc(acc_done, 1)
                            elif kk == 1 and t == TT - 1:
                                ins.then_inc(mm_done, 1)
                        if fresh == "x" and L == 0 and k < KT - PER:
                            for i in range(2):
                                first_item(k // PER + 1, 2 * (k % PER) + i)
                    if mod is not None:
                        if p == 0:
                            pe.wait_ge(mod_evac, mod[1])
                        pe.wait_ge(s_mw[p % 2], mod[0] * 128 + 32 * (p // 2 + 1))
                        mod_products(mod_w[:, p % 2], p, mod_used)
                    if rows is not None and p == 0:
                        pe.wait_ge(tr_free, tr_number(L, X, 0))
                        mod_transpose(*rows)
                    if kind in ("k", "q", "z") and 1 <= p <= TT:
                        if rows is not None and p == 2:
                            pe.wait_ge(ab_ready, rows[0] + 1)
                        stage_transposes(L, kind, X, p - 1)
                    if kind == "v" and p == 2:
                        pe.wait_ge(s_ck, 16 * (L + 1))
                        pe.wait_ge(tr_free, N_TR * L + TT)
                        for h in range(4):
                            ins = nc.tensor.transpose(bank[7][:, h * P:(h + 1) * P], stage[:, 0, h * P:(h + 1) * P], ident[:, :])
                        ins.then_inc(tr_done, 1)

            def h_transposes(L, kt):
                if kt % 4 == 0:
                    pe.wait_ge(x_normed, 4 * L + kt // 4 + 1)
                if kt > 0:
                    pe.wait_ge(h_ev, H0[L] + kt)
                if L == 0 or kt == 0:
                    pe.wait_ge(ab_ready, kt // PER + 1 if L == 0 else 2 * GROUPS)
                for t in range(TT):
                    dst = bank[6][:, t * P:(t + 1) * P] if t < TOK else bank[7][:, 0:P]
                    ins = nc.tensor.transpose(dst, x_tok[:, t, kt * P:(kt + 1) * P], ident[:, :])
                ins.then_inc(h_tr, 1)

            def stage_transposes(L, kind, X, t):
                n = tr_number(L, X, t)
                if kind == "z":
                    pe.wait_ge(acc_free, (X - 5) * TT + (TT * (14 * L + FIRST_Z) + t + 1))
                else:
                    pe.wait_ge(roped, X * TT + (25 * L + t + 1))
                if isinstance(X, int) and X == 0 and t == 0:
                    pe.wait_ge(h_ev, H0[L] + KT)
                elif t == 0:
                    pe.wait_ge(tr_free, n)
                elif not (isinstance(n, int) and n == 1):
                    pe.wait_ge(tr_free, n - 1)
                for h in range(4):
                    ins = nc.tensor.transpose(bank[6 + t % 2][:, h * P:(h + 1) * P], stage[:, t, h * P:(h + 1) * P], ident[:, :])
                ins.then_inc(tr_done, 1)

            for s in range(PAIRS):
                first_item(0, s)
            for L in range(LAYERS):
                chunk(L, 0, None, None, None if L == 0 else (6, 10), fresh="x")
                chunk(L, 1, "k", 0, (0, 4) if L == 0 else (7, 11))
                chunk(L, 2, "v", None, (1, 5) if L == 0 else None)
                with pe.Fori(1, 4) as i:
                    chunk(L, i + 2, "q", i, (i + 1, i + 5) if L == 0 else None,
                          rows=(i + 3, i + 4) if L == 0 else None)
                chunk(L, FIRST_Z, "q", 4, (5, 9) if L == 0 else None, rows=(7, 8) if L == 0 else None)
                with pe.Fori(1, 4) as i:
                    chunk(L, i + FIRST_Z, "z", i + 4)

                def scores_ready(gg, u):
                    U = unit(L, gg, u)
                    if isinstance(gg, int) and gg == 0 and u == 0:
                        pe.wait_ge(k_first, 2 * (L + 1))
                    else:
                        pe.wait_ge(q_split, U - L)
                        if u == 0:
                            pe.wait_ge(kv_main, gg * 2 + 7 * L)
                    if u == TOK:
                        pe.wait_ge(kv_req, gg * 2 + (8 * L + 1))

                def scores(gg, u, heads):
                    U, b = unit(L, gg, u), buf(u)
                    def product(out, h, col, n, stop=True):
                        q = slice(h * P, (h + 1) * P)
                        mm(out, q_hi[b][:, q], k_hi[:, col:col + n], start=True, stop=False)
                        mm(out, q_hi[b][:, q], k_lo[:, col:col + n], start=False, stop=False)
                        return mm(out, q_lo[b][:, q], k_hi[:, col:col + n], start=False, stop=stop)

                    if L == 1 and u < TOK and heads[0] == 0:
                        pe.wait_ge(exp_done, U * 4 + 4)
                        for h in range(4):
                            ins = product(bank[4][:, h * P:(h + 1) * P], h, CTX, P)
                        ins.then_inc(scx_done, 1)
                    parts = key_parts(L, u)
                    masks = []
                    if L == 0 and 0 < u < TOK:
                        masks.append((0, mask_prev))
                    if L == 0 and u < TOK - 1:
                        masks.append((P if u == 0 else 2 * P, mask_next))
                    for h in heads:
                        pe.wait_ge(exp_done, U * 4 + (h + 1))
                        if len(parts) == 2:
                            product(bank[h][:, parts[0][1]:parts[0][1] + P], h, parts[1][0], P)
                        ins = product(bank[h][:, 0:parts[0][1]], h, *parts[0], stop=not masks)
                        for n, (at, mask) in enumerate(masks):
                            ins = mm(bank[h][:, at:at + P], ident_b[:, :], mask[:, :], start=False,
                                     stop=(n == len(masks) - 1))
                        ins.then_inc(sc_done, 1)

                def probs_T(gg, u, kt):
                    table, done = (n_even, pt_act) if kt % 2 == 0 else (n_odd, pt_dve)
                    if kt == 0:
                        pe.wait_ge(pn_ready, unit(L, gg, u) + 1)
                    pe.wait_ge(done, before(table, L, gg, u) + (kt // 2 + 1))
                    for h in range(4):
                        ins = nc.tensor.transpose(bank[5 + kt % 2][:, h * P:(h + 1) * P],
                                                  probs[buf(u)][:, h, kt * P:(kt + 1) * P], ident[:, :])
                    ins.then_inc(pt_done, 1)

                def values(gg, u):
                    U, b, tiles = unit(L, gg, u), buf(u), key_tiles(L, u)
                    if u == 0:
                        pe.wait_ge(kv_main, gg * 2 + (7 * L + 1))
                    if u == TOK:
                        pe.wait_ge(kv_req, gg * 2 + (8 * L + 2))
                    pe.wait_ge(gated, U + CREDIT)
                    for kt, vt in enumerate(tiles):
                        done, table = (pt_act, n_even) if kt % 2 == 0 else (pt_dve, n_odd)
                        pe.wait_ge(done, before(table, L, gg, u) + (kt // 2 + 2))
                        ins = mm(bank[7][:, :], v_g[:, vt, :], probsT[b][:, kt, :], start=(kt == 0),
                                 stop=(kt == len(tiles) - 1))
                    ins.then_inc(o_done, 1)

                def pe_group(gg, last):
                    for u in range(TT):
                        tiles = list(range(n_kt[L][u]))
                        nxt = (gg, u + 1) if u < TOK else (gg + 1, 0)
                        more = not (last and u == TOK)
                        if more:
                            scores_ready(*nxt)
                        for h in range(4):
                            if more:
                                scores(*nxt, [h])
                            if tiles:
                                probs_T(gg, u, tiles.pop(0))
                        for kt in tiles:
                            probs_T(gg, u, kt)
                        values(gg, u)

                pe.wait_ge(acc_free, TT * (14 * L + FIRST_O))
                scores_ready(0, 0)
                scores(0, 0, range(4))
                for t in range(TT):
                    stage_transposes(L, "z", 8, t)
                pe.wait_ge(tr_free, N_TR * (L + 1))
                pe.wait_ge(mod_evac, 10 + 2 * L)
                with pe.Fori(0, 3) as gg:
                    pe_group(gg, False)
                pe_group(3, True)

                chunk(L, FIRST_O, None, None, fresh="o")
                with pe.Fori(1, 4) as n:
                    chunk(L, n + FIRST_O, None, None)


def rope_tables():
    n_tokens, grid_w, n_freq, theta = 512, 64, 32, 10000.0
    row, col = np.arange(n_tokens) // grid_w, np.arange(n_tokens) % grid_w
    inv = (np.float32(theta) ** (-np.arange(n_freq, dtype=np.float32) / n_freq)).astype(np.float32)
    ang = np.stack([row.astype(np.float32)[:, None] * inv, col.astype(np.float32)[:, None] * inv], axis=1)
    cos, sin = np.cos(ang).astype(np.float32), np.sin(ang).astype(np.float32)
    full_cos = np.stack([cos, cos], axis=2).reshape(n_tokens, 128)
    full_sin = np.stack([-sin, sin], axis=2).reshape(n_tokens, 128)
    return np.ascontiguousarray(full_cos), np.ascontiguousarray(full_sin)


_INS = ["x_prompt", "x_sample", "c", "cache_k", "cache_v", "c_ctx", "norm_g", "w_mod", "b_mod", "w_in",
        "q_norm_g", "k_norm_g", "sinks", "w_out"]
_OUTS = [("y_prompt", (1, 128, 2048)), ("y_sample", (1, 512, 2048)),
         ("new_cache_k", (1, 2, 128, 4, 128)), ("new_cache_v", (1, 2, 128, 4, 128))]


def kernel(**inputs):
    import concourse.bacc as bacc
    from concourse.bass_utils import run_bass_kernel_spmd

    nc = bacc.Bacc("TRN2", target_bir_lowering=False, num_devices=1)
    arrays = {f"in_{n}": np.ascontiguousarray(inputs[n]) for n in _INS}
    arrays["in_rope_cos"], arrays["in_rope_sin"] = rope_tables()
    args = [nc.dram_tensor(n, a.shape, mybir.dt.from_np(a.dtype), kind="ExternalInput").ap()
            for n, a in arrays.items()]
    args += [nc.dram_tensor(f"out_{n}", s, mybir.dt.float32, kind="ExternalOutput").ap() for n, s in _OUTS]
    build(nc, *args)
    r = run_bass_kernel_spmd(nc, [arrays], core_ids=[0])
    return tuple(r.results[0][f"out_{n}"] for n, _ in _OUTS)
```

```python
import numpy as np
import concourse.bass as bass
from concourse import mybir
from contextlib import ExitStack

P = 128
D = 2048
KT = D // P
TOK = 4
TT = TOK + 1
HEADS, KVH, GROUP = 16, 4, 4
NC = 512
PROJ = 5120
PAIRS = KT // 2
LAYERS = 2
N_CHUNKS = 14
FIRST_Z, FIRST_O = 6, 10
MODB = 1024
HALF = MODB // 2
GROUPS = D // HALF
PER = KT // GROUPS
RING0 = 7
BORDER0 = 3
BORDER_ITEMS = 4
EPS = 1e-6
SCALE = P ** -0.5
NEG = -1e30
CTX, REQ = TOK * P, TT * P
KCOLS = 6 * P
CREDIT = 5
N_TR = 46


def build(nc, x_prompt, x_sample, c, cache_k, cache_v, c_ctx, norm_g, w_mod, b_mod, w_in, q_norm_g,
          k_norm_g, sinks, w_out, rope_cos, rope_sin, y_prompt, y_sample, new_k, new_v):
    f32, f32r, bf16 = mybir.dt.float32, mybir.dt.float32r, mybir.dt.bfloat16
    ALU, ACT, AX = mybir.AluOpType, mybir.ActivationFunctionType, mybir.AxisListType.X
    ds = bass.ds
    ctx = ExitStack()
    with ctx:
        def sb(name, shape, dt=f32):
            return ctx.enter_context(nc.sbuf_tensor(name, shape, dt))

        def sem(name):
            return ctx.enter_context(nc.semaphore(name))

        gate_rows = nc.dram_tensor("gate_rows", [2, LAYERS * D], f32, kind="Internal").ap()
        z_spill = nc.dram_tensor("z_spill", [KVH - 1, TT, P, NC], f32, kind="Internal").ap()
        x_spill = nc.dram_tensor("x_spill", [TT, P, D], f32, kind="Internal").ap()

        def phase(*tensors):
            with ExitStack() as shared:
                return [shared.enter_context(nc.sbuf_tensor(*t)) for t in tensors]

        region = ("region", [P, 2 * KT * TT * P], f32)
        hT_hi, hT_lo = phase(*[(f"hT_{n}", [P, KT, TT * P], f32r) for n in ("hi", "lo")])
        tail = 12 * TT * P
        _, slot5, _, slot6 = phase(("pad0", [P, tail], f32), ("slot5", [P, 2, MODB], f32),
                                   ("pad1", [P, KT * TT * P - 2 * MODB], f32), ("slot6", [P, 2, MODB], f32))
        def halves(*names):
            return [(n, [P, NC], f32r) for n in names]

        (probs0, probs1, probs2, probsT0, probsT2, q_hi2, q_lo2, q_lo1, z_in, probsT1, v_g, k_hi, k_lo,
         q_hi0, q_lo0, q_hi1) = phase(
            ("probs0", [P, 4, 5 * P], f32), ("probs1", [P, 4, 5 * P], f32), ("probs2", [P, 4, P], f32),
            ("probsT0", [P, 5, NC], f32), ("probsT2", [P, 1, NC], f32), *halves("q_hi2", "q_lo2", "q_lo1"),
            ("z_in", [P, TT, NC], f32), ("probsT1", [P, 5, NC], f32), ("v_g", [P, 6, P], f32),
            ("k_hi", [P, KCOLS], f32r), ("k_lo", [P, KCOLS], f32r), *halves("q_hi0", "q_lo0", "q_hi1"))
        probs, probsT = (probs0, probs1, probs2), (probsT0, probsT1, probsT2)
        q_hi, q_lo = (q_hi0, q_hi1, q_hi2), (q_lo0, q_lo1, q_lo2)
        EARLY = 4
        ctx.enter_context(nc.sbuf_tensor(*region))

        qT_x = sb("qT_x", [P, KVH * TT * NC])
        qT = qT_x[:, :].rearrange("p (g t n) -> p g t n", g=KVH, t=TT)
        x_tok = qT_x[:, :].rearrange("p (t n) -> p t n", t=TT)
        kv = sb("kv", [P, 2 * KVH * KCOLS])
        kT = kv[:, 0:KVH * KCOLS].rearrange("p (g k) -> p g k", g=KVH)
        v_tok = kv[:, KVH * KCOLS:].rearrange("p (t n) -> p t n", t=6)
        w_raw = sb("w_raw", [P, 2, 2, NC])
        w_hi = sb("w_hi", [P, 2, 2, NC], f32r)
        w_lo = sb("w_lo", [P, 2, 2, NC], f32r)
        mod_ring = sb("mod_ring", [P, 2 * 2048])
        mod_w = mod_ring[:, :].rearrange("p (s k n) -> p s k n", s=2, k=2)
        first_ring = [kv[:, i * 2 * MODB:(i + 1) * 2 * MODB].rearrange("p (k n) -> p k n", k=2) for i in range(3)]
        first_ring += [mod_w[:, 0], mod_w[:, 1], slot5[:, :, :], slot6[:, :, :]]
        x_old = mod_ring[:, 0:TT * NC].rearrange("p (t n) -> p t n", t=TT)
        z_last = x_old
        gate = mod_ring[:, 2560:3584].rearrange("p (r n) -> p r n", r=2)
        gate_b = mod_ring[:, 3584:4096]
        stage = sb("stage", [P, TT, NC])
        h32 = stage[:, :, :].rearrange("p t n -> p (t n)")[:, 0:2 * TT * P].rearrange("p (s n) -> p s n", s=2)
        t1, t2 = sb("t1", [P, NC]), sb("t2", [P, NC])
        rope_c, rope_s = sb("rope_c", [P, TOK, P]), sb("rope_s", [P, TOK, P])
        gain = sb("gain", [P, P])
        mod_ev = sb("mod_ev", [P, MODB // 4])
        ident = sb("ident", [P, P])
        ident_b, mask_prev, mask_next = (sb(n, [P, P], bf16) for n in ("ident_b", "mask_prev", "mask_next"))
        consts = sb("consts", [P, P])
        rows = sb("rows", [P, P])
        cond = sb("cond", [P, KT, 2])
        mulA, addB = sb("mulA", [P, KT, 2]), sb("addB", [P, KT, 2])
        junk, eps = sb("junk", [P, P]), sb("eps", [P, 1])
        ss_x, ss_h = sb("ss_x", [P, TT, 4]), sb("ss_h", [P, TT, 4])
        rms_x, rms_h = sb("rms_x", [P, TT]), sb("rms_h", [P, TT, 4])
        sum_x, r_x, r_h = sb("sum_x", [P, TT]), sb("r_x", [P, TT]), sb("r_h", [P, 4])
        sink, neg_sink = sb("sink", [P, HEADS]), sb("neg_sink", [P, HEADS])
        mx, mxc, nmax, den, denx, sinkd, rden = (sb(n, [P, 4]) for n in
                                                 ("mx", "mxc", "nmax", "den", "denx", "sinkd", "rden"))
        bank = [ctx.enter_context(nc.psum_tensor(f"bank{i}", [P, 512], f32)) for i in range(8)]
        MODBANK = 5

        s_rows, s_x, s_sink = sem("s_rows"), [sem(f"s_x{i}") for i in range(TT)], sem("s_sink")
        s_first = [sem(f"s_first{i}") for i in range(RING0)]
        s_w = [sem(f"s_w{i}") for i in range(2)]
        s_mw = [sem(f"s_mw{i}") for i in range(2)]
        s_gate, s_tab, s_ck, s_cv, s_y3 = (sem(n) for n in ("s_gate", "s_tab", "s_ck", "s_cv", "s_y3"))
        s_newk, s_newv, s_y, s_last = (sem(n) for n in ("s_newk", "s_newv", "s_y", "s_last"))
        s_zout, s_zin = [sem(f"s_zout{i}") for i in range(2)], [sem(f"s_zin{i}") for i in range(TT)]
        s_old = sem("s_old")
        const_made, consts_T, consts_ready, cond_ready = (sem(n) for n in
                                                          ("const_made", "consts_T", "consts_ready", "cond_ready"))
        first_used, mod_used, mod_evac = sem("first_used"), sem("mod_used"), sem("mod_evac")
        kq_hi, k_first = sem("kq_hi"), sem("k_first")
        modT_done, ab_ready = sem("modT_done"), sem("ab_ready")
        xsq_done, x_normed, x_new, xsq_l1 = (sem(n) for n in ("xsq_done", "x_normed", "x_new", "xsq_l1"))
        x_summed, x_rooted = sem("x_summed"), sem("x_rooted")
        h_tr, h_ev, h_ready = sem("h_tr"), sem("h_ev"), sem("h_ready")
        whi_ready, wlo_ready, mm_done, acc_done, acc_free = (sem(n) for n in
                                                             ("whi_ready", "wlo_ready", "mm_done", "acc_done", "acc_free"))
        ss_ready, roped, tr_done, tr_free, tab_ready = (sem(n) for n in
                                                        ("ss_ready", "roped", "tr_done", "tr_free", "tab_ready"))
        gate_ready = sem("gate_ready")
        sc_done, nm_ready, exp_done, pn_ready = (sem(n) for n in ("sc_done", "nm_ready", "exp_done", "pn_ready"))
        scx_done, pt_done, pt_act, pt_dve = (sem(n) for n in ("scx_done", "pt_done", "pt_act", "pt_dve"))
        o_done, gated, q_split, kv_main, kv_req = (sem(n) for n in ("o_done", "gated", "q_split", "kv_main", "kv_req"))
        dve_chain, act_chain, pool_chain = sem("dve_chain"), sem("act_chain"), sem("pool_chain")

        class Chain:

            def __init__(self, s):
                self.s, self.base, self.k, self.i, self.per = s, 0, 0, 0, 0

            def link(self, eng, ins):
                ins.then_inc(self.s, 1)
                self.k += 1
                eng.wait_ge(self.s, self.i * self.per + (self.base + self.k) if self.per else self.base + self.k)

            def enter(self, i, first, per):
                self.base += self.k - first * per
                self.k, self.i, self.per = 0, i, per

            def leave(self, end):
                assert self.k == self.per, (self.k, self.per)
                self.base += end * self.per
                self.k, self.per = 0, 0

        def w_col(ch):
            return {0: 4096, 1: 4608}.get(ch) if isinstance(ch, int) and ch < 2 else (ch - 2) * NC

        def key_parts(L, u):
            if u == TOK:
                return [(REQ, P)]
            if L == 1:
                return [(0, NC)]
            lo, hi = max(0, u - 1) * P, min(TOK, u + 2) * P
            return [(lo, CTX + P - lo)] if hi == CTX else [(lo, hi - lo), (CTX, P)]

        def key_tiles(L, u):
            if u == TOK:
                return [5]
            if L == 1:
                return [0, 1, 2, 3, 4]
            return list(range(max(0, u - 1), min(TOK, u + 2))) + [4]

        n_kt = [[len(key_tiles(L, u)) for u in range(TT)] for L in range(LAYERS)]
        n_even = [[(n + 1) // 2 for n in row] for row in n_kt]
        n_odd = [[n // 2 for n in row] for row in n_kt]

        def before(table, L, g, u):
            return sum(4 * sum(table[l]) for l in range(L)) + g * sum(table[L]) + sum(table[L][:u])

        def unit(L, g, u):
            return g * TT + (20 * L + u)

        def same_buffer(L, g, u):
            return unit(L, g, u) - (TT if u == TOK else 2 if u >= 2 else 3)

        def n_between(L, u):
            if u == TOK:
                return n_kt[L][0:TOK]
            return [n_kt[L][u - 1]] if u >= 2 else [n_kt[L][3], n_kt[L][TOK]] if u == 0 else [n_kt[L][TOK], n_kt[L][0]]

        def attention(eng, step, chain=None, per=0):
            step(None, (0, 0), (0, 1))
            with eng.Fori(0, 3) as gg:
                if chain:
                    chain.enter(gg, 0, per)
                for u in range(1, TOK):
                    step((gg, u - 1), (gg, u), (gg, u + 1))
                step((gg, 3), (gg, TOK), (gg + 1, 0))
                step((gg, TOK), (gg + 1, 0), (gg + 1, 1))
                if chain:
                    chain.leave(3)
            for u in range(1, TT):
                step((3, u - 1), (3, u), (3, u + 1) if u < TOK else None)
            step((3, TOK), None, None)

        def short(prev):
            return prev is None or prev[1] == TOK

        def is_unit(x, g, u):
            return x is not None and isinstance(x[0], int) and tuple(x) == (g, u)

        Z_STORES = (3, 2)

        def buf(u):
            return 2 if u == TOK else u % 2

        def tr_number(L, X, t):
            return X * TT + (N_TR * L + t + (1 if not (isinstance(X, int) and X == 0) else 0))

        H0 = [0, 2 * KT]

        block = ctx.enter_context(nc.Block())

        @block.sync
        def _(sp):
            def mod_load(dst, L, kind, b, p, done):
                for kk in range(2):
                    rows = slice((2 * p + kk) * P, (2 * p + kk + 1) * P)
                    if kind == "S":
                        src = w_mod[L, rows, 0:2 * D].rearrange("p (s n) -> p s n", s=2)[:, :, ds(b * HALF, HALF)]
                        to = dst[:, kk, :].rearrange("p (s n) -> p s n", s=2)
                    else:
                        src, to = w_mod[L, rows, ds(b * MODB + 2 * D, MODB)], dst[:, kk, :]
                    sp.dma_start(to, src).then_inc(done, 16)

            def w_load(L, ch, src, n0, p):
                if not (isinstance(ch, int) and L == 0 and ch == 0 and p < 2):
                    sp.wait_ge(wlo_ready, (ch + 14 * L) * PAIRS + (p - 1))
                sp.dma_start(w_raw[:, p % 2], src[L, 2 * p * P:(2 * p + 2) * P, ds(n0, NC)]
                             .rearrange("(k p) n -> p k n", p=P)).then_inc(s_w[p % 2], 16)

            def chunk_loads(L, ch, src, n0, mod=None):
                for p in range(PAIRS):
                    w_load(L, ch, src, n0, p)
                    if L == 1 and isinstance(ch, int) and ch == 0 and p >= 1:
                        if p == 1:
                            sp.wait_ge(kv_main, 7)
                            sp.wait_ge(kv_req, 8)
                        for m in range(0 if p == 1 else min(PAIRS, BORDER_ITEMS + p - 1), min(PAIRS, BORDER_ITEMS + p)):
                            if m >= BORDER0:
                                sp.wait_ge(first_used, GROUPS * PAIRS + m - BORDER0 + 1)
                            mod_load(first_ring[m % BORDER0], 1, "G", 0, m, s_first[m % BORDER0])
                    if mod is not None:
                        number, ml, kind, b = mod
                        if isinstance(number, int) and number == 6 and p == 0:
                            sp.wait_ge(x_new, TT * 4)
                        if isinstance(number, int) and number == 0 and p < 2:
                            sp.wait_ge(first_used, GROUPS * PAIRS)
                        else:
                            sp.wait_ge(mod_used, number * PAIRS + (p - 1))
                        mod_load(mod_w[:, p % 2], ml, kind, b, p, s_mw[p % 2])

            for t in range(TT):
                src = x_sample[0, t * P:(t + 1) * P, :] if t < TOK else x_prompt[0]
                sp.dma_start(x_tok[:, t, :], src).then_inc(s_x[t], 16)
            for b in range(GROUPS):
                for p in range(PAIRS):
                    n = b * PAIRS + p
                    if n >= RING0:
                        sp.wait_ge(first_used, n - RING0 + 1)
                    mod_load(first_ring[n % RING0], 0, "S", b, p, s_first[n % RING0])
                for p in (2 * b, 2 * b + 1):
                    w_load(0, 0, w_in, w_col(0), p)

            for L in range(LAYERS):
                if L == 1:
                    chunk_loads(L, 0, w_in, w_col(0))
                chunk_loads(L, 1, w_in, w_col(1), (0, 0, "G", 0) if L == 0 else (6, 1, "G", 1))
                chunk_loads(L, 2, w_in, 0, (1, 1, "S", 0) if L == 0 else None)
                with sp.Fori(1, 4) as i:
                    chunk_loads(L, i + 2, w_in, i * NC, (i + 1, 1, "S", i) if L == 0 else None)
                chunk_loads(L, FIRST_Z, w_in, D, (5, 0, "G", 1) if L == 0 else None)
                with sp.Fori(1, 4) as i:
                    chunk_loads(L, i + FIRST_Z, w_in, i * NC + D, None)
                chunk_loads(L, FIRST_O, w_out, 0, None)
                with sp.Fori(1, 4) as i:
                    chunk_loads(L, i + FIRST_O, w_out, i * NC, None)

            for t in range(TT):
                sp.wait_ge(x_new, 20 + 3 * TT + t + 1)
                dst = y_sample[0, t * P:(t + 1) * P, 3 * NC:] if t < TOK else y_prompt[0, :, 3 * NC:]
                sp.dma_start(dst, x_tok[:, t, 3 * NC:]).then_inc(s_last, 16)
            sp.wait_ge(s_last, 16 * TT)

        @block.gpsimd
        def _(pool):
            chain = Chain(pool_chain)
            g = nc.gpsimd
            g.memset(eps[:], EPS)
            g.memset(mod_ev[:], 0.0)
            for t in (ident, ident_b, mask_prev, mask_next):
                chain.link(pool, g.memset(t[:], 0.0))
            for t in (ident, ident_b):
                chain.link(pool, g.affine_select(out=t[:], in_=t[:], compare_op=ALU.not_equal, fill=1.0, base=0,
                                                 pattern=[[-1, P]], channel_multiplier=1))
            chain.link(pool, g.affine_select(out=mask_prev[:], in_=mask_prev[:], compare_op=ALU.is_ge, fill=NEG,
                                             base=0, pattern=[[1, P]], channel_multiplier=-1))
            g.affine_select(out=mask_next[:], in_=mask_next[:], compare_op=ALU.is_ge, fill=NEG, base=0,
                            pattern=[[-1, P]], channel_multiplier=1).then_inc(const_made, 1)
            pool.dma_start(sink[:, :], sinks[0:1, :].to_broadcast([P, HEADS])).then_inc(s_sink, 16)

            def gate_store(n, Q):
                pool.wait_ge(mod_evac, Q + 1)
                for r in range(2):
                    pool.dma_start(gate_rows[r:r + 1, n * MODB:(n + 1) * MODB].rearrange("r (j n) -> (r j) n", j=4),
                                   mod_ev[r:r + 97:32, :]).then_inc(s_gate, 16)

            def table_loads(n, norm):
                if n > 0:
                    pool.wait_ge(roped, 5 if n == 1 else 25 if n == 2 else 30)
                pool.dma_start(rope_c[:, :, :], rope_cos.rearrange("(t p) d -> p t d", p=P)).then_inc(s_tab, 16)
                pool.dma_start(rope_s[:, :, :], rope_sin.rearrange("(t p) d -> p t d", p=P)).then_inc(s_tab, 16)
                pool.dma_start(gain[:, :], norm.to_broadcast([P, P])).then_inc(s_tab, 16)

            def z_stores(L, X):
                for t in range(TT):
                    pool.wait_ge(tr_free, tr_number(L, X, t) + 1)
                    pool.dma_start(z_spill[ds(X - 5, 1), t].rearrange("g p n -> (g p) n"),
                                   (t1, t2)[t % 2][:, :]).then_inc(s_zout[t % 2], 16)

            table_loads(0, k_norm_g[0:1, :])
            for L in range(LAYERS):
                if L == 1:
                    gate_store(2, 10)
                pool.wait_ge(roped, 25 * L + TT)
                pool.dma_start(new_k[0, L].rearrange("p h d -> p (h d)"), stage[:, TOK, :]).then_inc(s_newk, 16)
                pool.dma_start(v_tok[:, 4, :], cache_v[0, L].rearrange("p h d -> p (h d)")).then_inc(s_cv, 16)
                gate_store(*((0, 4) if L == 0 else (3, 11)))
                pool.wait_ge(tr_done, tr_number(L, 0, 4) + 1)
                pool.dma_start(stage[:, 0, :], cache_k[0, L].rearrange("p h d -> p (h d)")).then_inc(s_ck, 16)
                table_loads(2 * L + 1, q_norm_g[L:L + 1, :])
                pool.wait_ge(acc_free, (14 * L + 2) * TT)
                pool.dma_start(new_v[0, L].rearrange("p h d -> p (h d)"), v_tok[:, 5, :]).then_inc(s_newv, 16)
                if L == 0:
                    table_loads(2, k_norm_g[1:2, :])
                for X in (5, 6, 7):
                    z_stores(L, X)
                if L == 0:
                    gate_store(1, 9)

                def k_split(gg, first, n, prev, done):
                    pool.wait_ge(sc_done, prev * 4 + (4 * CREDIT + 4))
                    src = kT[:, ds(gg, 1), first:first + n].rearrange("p g k -> p (g k)")
                    g.tensor_copy(k_hi[:, first:first + n], src)
                    pool.drain()
                    g.tensor_tensor(k_lo[:, first:first + n], src, k_hi[:, first:first + n].bitcast(f32),
                                    ALU.subtract).then_inc(done, 1)

                def v_copy(gg, first, n, prev, done):
                    pool.wait_ge(o_done, prev + (CREDIT + 1))
                    g.tensor_copy(v_g[:, first // P:(first + n) // P, :],
                                  v_tok[:, first // P:(first + n) // P, ds(gg * P, P)]).then_inc(done, 1)

                def q_split_unit(gg, u):
                    U, prev = unit(L, gg, u), same_buffer(L, gg, u)
                    pool.wait_ge(sc_done, prev * 4 + (4 * CREDIT + 4))
                    src = qT[:, ds(gg, 1), u, :].rearrange("p g n -> p (g n)")
                    g.tensor_copy(q_hi[buf(u)][:, :], src)
                    pool.drain()
                    g.tensor_tensor(q_lo[buf(u)][:, :], src, q_hi[buf(u)][:, :].bitcast(f32), ALU.subtract).then_inc(q_split, 1)

                def z_load(gg, u):
                    pool.wait_ge(gated, unit(L, gg, u) + (CREDIT - TT + 1))
                    pool.dma_start(z_in[:, u, :], z_spill[ds(gg, 1), u].rearrange("g p n -> (g p) n")
                                   ).then_inc(s_zin[u], 16)

                pool.wait_ge(acc_done, (14 * L + FIRST_O) * TT)
                pool.wait_ge(tr_free, tr_number(L, 4, 4) + 1)
                pool.wait_ge(s_cv, 16 * (L + 1))
                for i in range(2):
                    pool.wait_ge(s_zout[i], 48 * Z_STORES[i] * (L + 1))

                def pool_group(gg, last):
                    for u in range(TT):
                        if u < TOK:
                            q_split_unit(gg, u + 1)
                        elif not last:
                            k_split(gg + 1, 0, 5 * P, unit(L, gg, 3), kv_main)
                            q_split_unit(gg + 1, 0)
                        if not last:
                            z_load(gg, u)
                        if u == 0:
                            v_copy(gg, 0, 5 * P, unit(L, gg, 0) - 2, kv_main)
                            k_split(gg, REQ, P, unit(L, gg, 0) - 1, kv_req)
                            v_copy(gg, REQ, P, unit(L, gg, 0) - 1, kv_req)

                with pool.Fori(0, 3) as gg:
                    pool_group(gg, False)
                pool_group(3, True)

                def out_loads(n):
                    if isinstance(n, int) and n == 0:
                        pool.wait_ge(gated, CREDIT + 20 * (L + 1))
                        pool.wait_ge(s_gate, 64 * (L + 1))
                        if L == 1:
                            pool.wait_ge(s_y, 16 * TT * 3)
                            pool.wait_ge(s_y3, 16 * TT)
                    else:
                        pool.wait_ge(x_new, n * TT + 20 * L)
                    for t in range(TT):
                        if L == 1:
                            src = x_spill[t, :, ds(n * NC, NC)]
                        elif t < TOK:
                            src = x_sample[0, t * P:(t + 1) * P, ds(n * NC, NC)]
                        else:
                            src = x_prompt[0, :, ds(n * NC, NC)]
                        pool.dma_start(x_old[:, t, :], src).then_inc(s_old, 16)
                    col = n * NC + D * L
                    for r in range(2):
                        pool.dma_start(gate[:, r, :], gate_rows[r:r + 1, ds(col, NC)].to_broadcast([P, NC])
                                       ).then_inc(s_old, 16)
                    pool.dma_start(gate_b, b_mod[L:L + 1, ds(n * NC + 2 * D, NC)].to_broadcast([P, NC])
                                   ).then_inc(s_old, 16)

                def out_stores(n, done):
                    for t in range(TT):
                        pool.wait_ge(x_new, n * TT + (20 * L + t + 1))
                        if L == 0:
                            dst = x_spill[t, :, ds(n * NC, NC)]
                        elif t < TOK:
                            dst = y_sample[0, t * P:(t + 1) * P, ds(n * NC, NC)]
                        else:
                            dst = y_prompt[0, :, ds(n * NC, NC)]
                        pool.dma_start(dst, x_tok[:, t, ds(n * NC, NC)]).then_inc(done, 16)

                out_loads(0)
                out_stores(0, s_y)
                with pool.Fori(1, 3) as n:
                    out_loads(n)
                    out_stores(n, s_y)
                out_loads(3)
                if L == 0:
                    out_stores(3, s_y3)

            pool.wait_ge(s_newk, 16 * LAYERS)
            pool.wait_ge(s_newv, 16 * LAYERS)
            pool.wait_ge(s_y, 16 * TT * 3 * LAYERS)
            pool.wait_ge(s_y3, 16 * TT)
            pool.wait_ge(s_gate, 64 * LAYERS)
            for i in range(2):
                pool.wait_ge(s_zout[i], 48 * Z_STORES[i] * LAYERS)

        @block.scalar
        def _(act):
            chain = Chain(act_chain)
            s = nc.scalar
            act.dma_start(rows[0:16, :], c.rearrange("a (j p) -> (a j) p", p=P)).then_inc(s_rows, 16)
            act.dma_start(rows[16:32, :], c_ctx.rearrange("(j p) -> j p", p=P)).then_inc(s_rows, 16)
            act.dma_start(rows[32:64, :], norm_g.rearrange("l (j p) -> (l j) p", p=P)).then_inc(s_rows, 16)
            for L in range(LAYERS):
                act.dma_start(rows[64 + 32 * L:96 + 32 * L, :],
                               b_mod[L, 0:2 * D].rearrange("(j p) -> j p", p=P)).then_inc(s_rows, 16)
            act.wait_ge(consts_ready, 1)
            s.activation(cond[:, :, :].rearrange("p k r -> p r k"), consts[:, 0:32].rearrange("p (r k) -> p r k", r=2),
                         ACT.Silu).then_inc(cond_ready, 1)

            def first_squares():
                for t in range(TT):
                    act.wait_ge(s_x[t], 16)
                    ins = s.activation(stage[:, 0:4, :].rearrange("p t n -> p (t n)"), x_tok[:, t, :], ACT.Square,
                                       accum_out=ss_x[:, t, 0:1])
                    if t == TT - 1:
                        ins.then_inc(xsq_done, 1)
                    else:
                        chain.link(act, ins)

            def mod_evacuate(used, count, transposed=None, stored=None):
                act.wait_ge(used, count)
                if transposed is not None:
                    act.wait_ge(modT_done, transposed)
                if stored is not None:
                    act.wait_ge(s_gate, stored)
                for j in range(4):
                    ins = s.copy(mod_ev[32 * j:32 * j + 2, :], bank[MODBANK][32 * j:32 * j + 2, 0:256])
                ins.then_inc(mod_evac, 1)

            def split_hi(L, ch, p):
                C = ch + 14 * L
                act.wait_ge(s_w[p % 2], C * 64 + 16 * (p // 2 + 1))
                start = isinstance(ch, int) and L == 0 and ch == 0
                if p == 0 and not start:
                    act.wait_ge(mm_done, C * 7)
                elif p == 1 and not start:
                    act.wait_ge(acc_done, C * TT)
                elif p >= 2:
                    act.wait_ge(mm_done, C * 7 + (p - 1))
                s.copy(w_hi[:, p % 2], w_raw[:, p % 2]).then_inc(whi_ready, 1)

            def evacuate(L, ch, kind, X):
                C = ch + 14 * L
                for t in range(TT):
                    act.wait_ge(acc_done, C * TT + (t - 4))
                    if kind == "v":
                        s.copy(v_tok[:, t if t < TOK else 5, :], bank[t][:, :]).then_inc(acc_free, 1)
                        continue
                    if kind == "k":
                        act.wait_ge(h_ready, H0[L] + KT)
                    else:
                        act.wait_ge(tr_done, X * TT + (N_TR * L + t - TT + 2))
                    s.activation(stage[:, t, :], bank[t][:, :], ACT.Silu if kind == "z" else ACT.Copy
                                 ).then_inc(acc_free, 1)

            def head_squares(L, X):
                R = X * TT + 25 * L
                if not (isinstance(X, int) and X == 0 and L == 0):
                    act.wait_ge(roped, R)
                act.wait_ge(acc_free, (14 * L + 1 + X + (0 if isinstance(X, int) and X == 0 else 1)) * TT)
                for t in range(TT):
                    for h in range(4):
                        chain.link(act, s.activation(junk[:, :], stage[:, t, h * P:(h + 1) * P], ACT.Square,
                                                     accum_out=ss_h[:, t, h:h + 1]))
                    s.activation(rms_h[:, t, :], ss_h[:, t, :], ACT.Sqrt, bias=eps[:, :], scale=1.0 / P
                                 ).then_inc(ss_ready, 1)

            def evac_transposed(L, kind, X, t):
                n = tr_number(L, X, t)
                act.wait_ge(tr_done, n + 1)
                src = bank[6 + t % 2]
                if kind == "k":
                    col = t * P if t < TOK else REQ
                    dst, src = kT[:, :, col:col + P], src[:, :].rearrange("p (g n) -> p g n", g=4)
                elif kind == "q":
                    dst, src = qT[:, ds(X - 1, 1), t, :].rearrange("p g n -> p (g n)"), src[:, :]
                elif isinstance(X, int) and X == 8:
                    dst, src = z_last[:, t, :], src[:, :]
                else:
                    if isinstance(X, int) and X == 5 and t < 2:
                        act.wait_ge(roped, 25 * (L + 1))
                    if not (isinstance(X, int) and X == 5 and t < 2 and L == 0):
                        act.wait_ge(s_zout[t % 2], (X - 5) * (16 * Z_STORES[t % 2]) + (48 * Z_STORES[t % 2] * L + 16 * (t // 2)))
                    dst, src = (t1, t2)[t % 2][:, :], src[:, :]
                s.copy(dst, src).then_inc(tr_free, 1)

            def h_evacuate(L, kt):
                act.wait_ge(h_tr, KT * L + kt + 1)
                if kt >= 2:
                    act.wait_ge(h_ready, H0[L] + kt - 1)
                elif kt == 0:
                    act.wait_ge(ab_ready, L + 1)
                    act.wait_ge(*((xsq_done, 1) if L == 0 else (xsq_l1, 20 + TT)))
                s.activation(h32[:, kt % 2, 0:NC], bank[6][:, :], ACT.Identity,
                             bias=addB[:, kt, 0:1], scale=mulA[:, kt, 0:1])
                s.activation(h32[:, kt % 2, NC:NC + P], bank[7][:, 0:P], ACT.Identity,
                             bias=addB[:, kt, 1:2], scale=mulA[:, kt, 1:2]).then_inc(h_ev, 1)

            def gated_hi(L, kt):
                if kt % 4 == 0 and kt < 3 * GROUP:
                    act.wait_ge(gated, CREDIT + 20 * L + TT * (kt // 4 + 1))
                src = qT[:, kt // 4, :, (kt % 4) * P:(kt % 4 + 1) * P]
                s.copy(hT_hi[:, kt, :].rearrange("p (t n) -> p t n", t=TT), src).then_inc(h_ev, 1)

            def chunk(L, ch, kind, X, mod=None):
                split_hi(L, ch, 0)
                if kind in ("k", "v", "q", "z"):
                    evacuate(L, ch, kind, X)
                split_hi(L, ch, 1)
                if mod is not None:
                    mod_evacuate(*mod)
                if kind in ("k", "q"):
                    head_squares(L, X)
                for p in range(2, PAIRS):
                    split_hi(L, ch, p)
                    if kind in ("k", "q", "z") and p - 2 < TT:
                        evac_transposed(L, kind, X, p - 2)
                    if kind == "v" and p == 3:
                        act.wait_ge(tr_done, N_TR * L + TT + 1)
                        s.copy(kT[:, :, CTX:CTX + P], bank[7][:, :].rearrange("p (g n) -> p g n", g=4)
                               ).then_inc(tr_free, 1)
                    if kind == "o" and L == 0 and p - 2 < TT:
                        new_square(ch - FIRST_O - 1, p - 2)

            def new_square(n, t):
                act.wait_ge(x_new, n * TT + (t + 1))
                s.activation(stage[:, t, :], x_tok[:, t, ds(n * NC, NC)], ACT.Square,
                             accum_out=ss_x[:, t, ds(n, 1)]).then_inc(xsq_l1, 1)

            for L in range(LAYERS):
                def x_root():
                    act.wait_ge(x_summed, L + 1)
                    s.activation(rms_x[:, :], sum_x[:, :], ACT.Sqrt, bias=eps[:, :], scale=1.0 / D).then_inc(x_rooted, 1)

                if L == 0:
                    act.wait_ge(const_made, 1)
                    first_squares()
                    x_root()
                    for b in range(GROUPS):
                        mod_evacuate(first_used, (b + 1) * PAIRS, transposed=b or None)
                        for kt in range(PER * b, PER * b + PER):
                            if kt % 2 == 0:
                                split_hi(0, 0, kt // 2)
                            h_evacuate(0, kt)
                else:
                    x_root()
                    for p in range(PAIRS):
                        if p:
                            split_hi(L, 0, p)
                        for kt in (2 * p, 2 * p + 1):
                            h_evacuate(L, kt)
                chunk(L, 1, "k", 0, None if L == 0 else (first_used, (GROUPS + 1) * PAIRS, 8, 64))
                chunk(L, 2, "v", None, (mod_used, PAIRS, 4, None) if L == 0 else (mod_used, 7 * PAIRS, None, 96))
                act.wait_ge(s_newk, 16 * (L + 1))
                with act.Fori(1, 4) as i:
                    chain.enter(i, 1, 4 * TT)
                    chunk(L, i + 2, "q", i, (mod_used, i * PAIRS + PAIRS, i + 3, 32) if L == 0 else None)
                    chain.leave(4)
                chunk(L, FIRST_Z, "q", 4, (mod_used, 5 * PAIRS, 7, 32) if L == 0 else None)
                with act.Fori(1, 4) as i:
                    chunk(L, i + FIRST_Z, "z", i + 4)
                if L == 0:
                    mod_evacuate(mod_used, 6 * PAIRS, 8)
                act.wait_ge(mm_done, (14 * L + FIRST_O) * 7)
                act.wait_ge(tr_free, tr_number(L, 4, 4) + 1)
                s.copy(k_hi[:, 0:5 * P], kT[:, 0, 0:5 * P])
                s.copy(q_hi[0][:, :], qT[:, 0, 0, :]).then_inc(kq_hi, 1)
                evacuate(L, FIRST_O, "z", 8)

                def exps(gg, u, h):
                    U = unit(L, gg, u)
                    b, n = buf(u), P * n_kt[L][u]
                    if h % 2 == 0:
                        act.wait_ge(nm_ready, U * 2 + (h // 2 + 1))
                    if h == 0 and not (isinstance(gg, int) and gg == 0 and L == 0):
                        act.wait_ge(pt_done, before(n_kt, L, gg, u) - sum(n_between(L, u)))
                    m = min(n, NC)
                    ins = s.activation(probs[b][:, h, 0:m], bank[h][:, 0:m], ACT.Exp, bias=nmax[:, h:h + 1],
                                       scale=SCALE, accum_out=den[:, h:h + 1])
                    if n > NC:
                        ins = s.activation(probs[b][:, h, NC:n], bank[4][:, h * P:(h + 1) * P], ACT.Exp,
                                           bias=nmax[:, h:h + 1], scale=SCALE, accum_out=denx[:, h:h + 1])
                    if L == 0 and h == 3:
                        ins = s.activation(denx[:, :], sinkd[:, :], ACT.Exp)
                    ins.then_inc(exp_done, 1)

                def probs_out(gg, u, kt):
                    U, prev = unit(L, gg, u), same_buffer(L, gg, u)
                    act.wait_ge(pt_done, before(n_kt, L, gg, u) + (kt + 1))
                    if kt == 0:
                        act.wait_ge(o_done, prev + (CREDIT + 1))
                    s.copy(probsT[buf(u)][:, kt, :], bank[5 + kt % 2][:, :]).then_inc(pt_act, 1)

                def act_step(prev, now, nxt):
                    even = list(range(0, n_kt[L][now[1]], 2)) if now else []
                    if is_unit(now, 3, 2):
                        split_hi(L, FIRST_O, 0)
                    if is_unit(now, 3, 3):
                        act.wait_ge(pt_done, before(n_kt, L, 3, 3))
                        gated_hi(L, 0)
                        gated_hi(L, 1)
                    if is_unit(now, 3, TOK):
                        gated_hi(L, 2)
                        gated_hi(L, 3)
                    for h in range(4):
                        if even and nxt and short(prev) and h in (0, 1, 3):
                            probs_out(*now, even.pop(0))
                        if nxt:
                            exps(*nxt, h)
                        if even and h > 0 and not (nxt and short(prev)):
                            probs_out(*now, even.pop(0))

                exps(0, 0, 0)
                exps(0, 0, 1)
                evac_transposed(L, "z", 8, 0)
                evac_transposed(L, "z", 8, 1)
                exps(0, 0, 2)
                exps(0, 0, 3)
                for t in range(2, TT):
                    evac_transposed(L, "z", 8, t)
                attention(act, act_step)

                if L == 0:
                    chain.link(act, s.activation(junk[:, 0:1], eps[:, :], ACT.Sqrt))
                for p in range(1, PAIRS):
                    split_hi(L, FIRST_O, p)
                    for kt in (2 * p, 2 * p + 1):
                        if kt == EARLY:
                            act.wait_ge(o_done, CREDIT + 20 * (L + 1))
                        if kt == 3 * GROUP:
                            act.wait_ge(gated, CREDIT + 20 * (L + 1))
                        if kt >= EARLY:
                            gated_hi(L, kt)
                with act.Fori(1, 4) as n:
                    chunk(L, n + FIRST_O, "o", None)
                if L == 0:
                    split_hi(1, 0, 0)
                    for t in range(TT):
                        new_square(3, t)

        @block.vector
        def _(dve):
            chain = Chain(dve_chain)
            v = nc.vector
            dve.wait_ge(consts_T, 1)
            v.tensor_copy(consts[:, :], bank[7][:, 0:P]).then_inc(consts_ready, 1)

            def x_norm(L):
                if L == 0:
                    dve.wait_ge(xsq_done, 1)
                    v.tensor_copy(sum_x[:, :], ss_x[:, :, 0:1].rearrange("p t n -> p (t n)")).then_inc(x_summed, 1)
                else:
                    dve.wait_ge(xsq_l1, 20 + TT)
                    v.tensor_reduce(sum_x[:, :], ss_x[:, :, :], AX, ALU.add).then_inc(x_summed, 1)
                dve.wait_ge(x_rooted, L + 1)
                chain.link(dve, v.reciprocal(r_x[:, :], rms_x[:, :]))
                for n in range(4):
                    if L == 0 and n == 0:
                        for t in range(TT):
                            dve.wait_ge(s_x[t], 16)
                    if L == 0 or n == 0:
                        x_scale(L, n)

            def x_scale(L, n):
                if L == 1 and n == 0:
                    dve.wait_ge(s_y, 16 * TT * 3)
                if L == 1 and n == 3:
                    dve.wait_ge(s_y3, 16 * TT)
                for t in range(TT):
                    v.tensor_scalar(x_tok[:, t, n * NC:(n + 1) * NC], x_tok[:, t, n * NC:(n + 1) * NC],
                                    r_x[:, t:t + 1], None, ALU.mult).then_inc(x_normed, 1)

            def scale_shift(L, b):
                dve.wait_ge(modT_done, b + (GROUPS * L + 1))
                src = bank[7][:, 0:256].rearrange("p (s j r) -> p j s r", s=2, j=4)
                at = b * PER

                def both(a):
                    return a.rearrange("p (j s r) -> p j s r", s=2, r=1).to_broadcast([P, 2, 2, 2])

                def part(t):
                    return t[:, ds(at, PER), :].rearrange("p (j s) r -> p j s r", s=2)

                v.tensor_tensor(part(addB), src[:, 0:2, :, 0:2], both(consts[:, ds(at + (64 + 32 * L), PER)]), ALU.add)
                chain.link(dve, v.tensor_tensor(part(mulA), src[:, 2:4, :, 0:2],
                                                both(consts[:, ds(at + (64 + 32 * L + KT), PER)]), ALU.add))
                v.scalar_tensor_tensor(part(mulA), part(mulA), 1.0, both(consts[:, ds(at + (32 + 16 * L), PER)]),
                                       ALU.add, ALU.mult).then_inc(ab_ready, 1)

            def tables(n):
                dve.wait_ge(s_tab, 48 * (n + 1))
                gb = gain[:, :].rearrange("p (t d) -> p t d", t=1).to_broadcast([P, TOK, P])
                chain.link(dve, v.tensor_tensor(rope_c[:, :, :], rope_c[:, :, :], gb, ALU.mult))
                for a in range(2):
                    for hf in range(2):
                        o, other = 64 * a + 32 * hf, 64 * a + 32 * (1 - hf)
                        gs = gain[:, other:other + 32].rearrange("p (t d) -> p t d", t=1).to_broadcast([P, TOK, 32])
                        ins = v.tensor_tensor(rope_s[:, :, o:o + 32], rope_s[:, :, o:o + 32], gs, ALU.mult)
                chain.link(dve, ins)

            def split_lo(L, ch, p):
                C = ch + 14 * L
                dve.wait_ge(whi_ready, C * PAIRS + (p + 1))
                dve.wait_ge(s_w[p % 2], C * 64 + 16 * (p // 2 + 1))
                v.tensor_tensor(w_lo[:, p % 2], w_raw[:, p % 2], w_hi[:, p % 2].bitcast(f32),
                                ALU.subtract).then_inc(wlo_ready, 1)

            def norm_rope(L, X, t):
                R = X * TT + (25 * L + t)
                dve.wait_ge(ss_ready, R + 1)
                chain.link(dve, v.reciprocal(r_h[:, :], rms_h[:, t, :]))
                st = stage[:, t, :].rearrange("p (h d) -> p h d", h=4)
                rb = r_h[:, :].rearrange("p (h d) -> p h d", d=1).to_broadcast([P, 4, P])
                chain.link(dve, v.tensor_tensor(st, st, rb, ALU.mult))
                if t == TOK:
                    gb = gain[:, :].rearrange("p (h d) -> p h d", h=1).to_broadcast([P, 4, P])
                    v.tensor_tensor(st, st, gb, ALU.mult).then_inc(roped, 1)
                    dve.wait_ge(roped, R + 1)
                    return
                a1 = t1[:, :].rearrange("p (h d) -> p h d", h=4)
                a2 = t2[:, :].rearrange("p (ha f d) -> p ha f d", f=2, d=32)
                sf = stage[:, t, :].rearrange("p (ha f d) -> p ha f d", f=2, d=32)
                cb = rope_c[:, t:t + 1, :].to_broadcast([P, 4, P])
                v.tensor_tensor(a1, st, cb, ALU.mult)
                for hf in range(2):
                    for a in range(2):
                        o = 64 * a + 32 * hf
                        x_other = stage[:, t, :].rearrange("p (h d) -> p h d", h=4)[:, :, 64 * a + 32 * (1 - hf):64 * a + 32 * (1 - hf) + 32]
                        dst = t2[:, :].rearrange("p (h d) -> p h d", h=4)[:, :, o:o + 32]
                        ins = v.tensor_tensor(dst, x_other, rope_s[:, t:t + 1, o:o + 32].to_broadcast([P, 4, 32]), ALU.mult)
                chain.link(dve, ins)
                v.tensor_tensor(stage[:, t, :], t1[:, :], t2[:, :], ALU.add).then_inc(roped, 1)
                dve.wait_ge(roped, R + 1)

            LINKS_Q = 2 * TT + TOK

            def gate_add(L, n):
                dve.wait_ge(s_old, (n * 128 + 128 * (4 * L + 1)) if not isinstance(n, int) else 128 * (4 * L + n + 1))
                for_both = gate_b.rearrange("p (r n) -> p r n", r=1).to_broadcast([P, 2, NC])
                chain.link(dve, v.tensor_tensor(gate, gate, for_both, ALU.add))

            def gate_out(L, n, t):
                dve.wait_ge(acc_done, n * TT + (TT * (14 * L + FIRST_O) + t + 1))
                if L == 0:
                    dve.wait_ge(xsq_l1, n * TT + (t + 1))
                v.tensor_tensor(stage[:, t, :], bank[t][:, :], gate[:, 0 if t < TOK else 1, :],
                                ALU.mult).then_inc(acc_free, 1)

            def add_x(L, n, t):
                dve.wait_ge(acc_free, n * TT + (TT * (14 * L + FIRST_O) + t + 1))
                v.tensor_tensor(x_tok[:, t, ds(n * NC, NC)], stage[:, t, :], x_old[:, t, :],
                                ALU.add).then_inc(x_new, 1)

            def chunk(L, ch, kind, X, mod=None):
                split_lo(L, ch, 0)
                if kind == "o":
                    gate_add(L, ch - FIRST_O - 1)
                    for t in range(TT):
                        gate_out(L, ch - FIRST_O - 1, t)
                split_lo(L, ch, 1)
                if mod is not None:
                    scale_shift(1, mod)
                for p in range(2, PAIRS):
                    if p - 2 < TT:
                        if kind in ("k", "q"):
                            norm_rope(L, X, p - 2)
                        if kind == "o":
                            add_x(L, ch - FIRST_O - 1, p - 2)
                    split_lo(L, ch, p)

            for L in range(LAYERS):
                def h_split(kt):
                    dve.wait_ge(h_ev, H0[L] + kt + 1)
                    chain.link(dve, v.tensor_copy(hT_hi[:, kt, :], h32[:, kt % 2, :]))
                    v.tensor_tensor(hT_lo[:, kt, :], h32[:, kt % 2, :], hT_hi[:, kt, :].bitcast(f32),
                                    ALU.subtract).then_inc(h_ready, 1)

                if L == 0:
                    dve.wait_ge(consts_ready, 1)
                    x_norm(0)
                    for b in range(GROUPS):
                        scale_shift(0, b)
                        if b == GROUPS - 1:
                            dve.wait_ge(first_used, GROUPS * PAIRS)
                        for kt in range(PER * b, PER * b + PER):
                            if kt % 2 == 0:
                                split_lo(0, 0, kt // 2)
                            h_split(kt)
                else:
                    split_lo(L, 0, 0)
                    x_norm(1)
                    dve.wait_ge(acc_done, 14 * TT)
                    for p in range(PAIRS):
                        if p:
                            split_lo(L, 0, p)
                        for kt in (2 * p, 2 * p + 1):
                            h_split(kt)
                            if kt % 4 == 0 and kt < 12:
                                x_scale(1, kt // 4 + 1)
                if L == 0:
                    dve.wait_ge(s_sink, 16)
                    chain.link(dve, v.tensor_scalar(neg_sink[:, :], sink[:, :], -1.0, None, ALU.mult))
                    tables(0)
                chunk(L, 1, "k", 0)
                split_lo(L, 2, 0)
                split_lo(L, 2, 1)
                tables(2 * L + 1)
                for p in range(2, PAIRS):
                    split_lo(L, 2, p)
                with dve.Fori(1, 4) as i:
                    chain.enter(i, 1, LINKS_Q + (1 if L == 0 else 0))
                    chunk(L, i + 2, "q", i, i - 1 if L == 0 else None)
                    chain.leave(4)
                chunk(L, FIRST_Z, "q", 4, 3 if L == 0 else None)
                with dve.Fori(1, 4) as i:
                    chunk(L, i + FIRST_Z, None, None)
                if L == 0:
                    tables(2)

                def ctx_maxima(gg, u):
                    dve.wait_ge(scx_done, gg * TOK + (u + 1))
                    return v.tensor_reduce(mxc[:, :], bank[4][:, :].rearrange("p (h k) -> p h k", h=4), AX, ALU.max)

                def maxima(gg, u, h0):
                    U, n, hs = unit(L, gg, u), P * n_kt[L][u], slice(h0, h0 + 2)
                    for h in (h0, h0 + 1):
                        dve.wait_ge(sc_done, U * 4 + (4 * CREDIT + h + 1))
                        ins = v.tensor_reduce(mx[:, h:h + 1], bank[h][:, 0:min(n, NC)], AX, ALU.max)
                    if n > NC and h0 == 0:
                        ins = ctx_maxima(gg, u)
                    chain.link(dve, ins)
                    if n > NC:
                        chain.link(dve, v.tensor_tensor(mx[:, hs], mx[:, hs], mxc[:, hs], ALU.max))
                    if L == 1:
                        v.tensor_scalar(nmax[:, hs], mx[:, hs], -SCALE, None, ALU.mult).then_inc(nm_ready, 1)
                    else:
                        chain.link(dve, v.scalar_tensor_tensor(nmax[:, hs], mx[:, hs], -SCALE,
                                                               neg_sink[:, ds(gg * 4 + h0, 2)], ALU.mult, ALU.min))
                        v.tensor_tensor(sinkd[:, hs], nmax[:, hs], sink[:, ds(gg * 4 + h0, 2)], ALU.add
                                        ).then_inc(nm_ready, 1)

                def normalise(gg, u):
                    U, b, n = unit(L, gg, u), buf(u), P * n_kt[L][u]
                    dve.wait_ge(exp_done, U * 4 + 8)
                    if L == 0 or n > NC:
                        chain.link(dve, v.tensor_tensor(rden[:, :], den[:, :], denx[:, :], ALU.add))
                        chain.link(dve, v.reciprocal(rden[:, :], rden[:, :]))
                    else:
                        chain.link(dve, v.reciprocal(rden[:, :], den[:, :]))
                    for h in range(4):
                        ins = v.tensor_scalar(probs[b][:, h, 0:n], probs[b][:, h, 0:n], rden[:, h:h + 1], None, ALU.mult)
                    ins.then_inc(pn_ready, 1)

                def probs_out(gg, u, kt):
                    U, prev = unit(L, gg, u), same_buffer(L, gg, u)
                    dve.wait_ge(pt_done, before(n_kt, L, gg, u) + (kt + 1))
                    if kt == 1:
                        dve.wait_ge(o_done, prev + (CREDIT + 1))
                    v.tensor_copy(probsT[buf(u)][:, kt, :], bank[5 + kt % 2][:, :]).then_inc(pt_dve, 1)

                def gate_unit(gg, u):
                    U = unit(L, gg, u)
                    dve.wait_ge(o_done, U + (CREDIT + 1))
                    last = isinstance(gg, int) and gg == 3
                    if last:
                        dve.wait_ge(tr_free, N_TR * (L + 1))
                    else:
                        dve.wait_ge(s_zin[u], gg * 16 + 16 * (3 * L + 1))
                    if not (isinstance(gg, int) and gg == 0 and u == 0):
                        dve.wait_ge(q_split, U - L)
                    dst = qT[:, ds(gg, 1), u, :].rearrange("p g n -> p (g n)")
                    v.tensor_tensor(dst, bank[7][:, :], (z_last if last else z_in)[:, u, :], ALU.mult).then_inc(gated, 1)

                def gated_lo(kt):
                    dve.wait_ge(h_ev, H0[L] + KT + kt + 1)
                    src = qT[:, kt // 4, :, (kt % 4) * P:(kt % 4 + 1) * P]
                    v.tensor_tensor(hT_lo[:, kt, :].rearrange("p (t n) -> p t n", t=TT), src,
                                    hT_hi[:, kt, :].bitcast(f32).rearrange("p (t n) -> p t n", t=TT),
                                    ALU.subtract).then_inc(h_ready, 1)

                def dve_step(prev, now, nxt):
                    odd = list(range(1, n_kt[L][now[1]], 2)) if now else []
                    if is_unit(now, 3, 2):
                        split_lo(L, FIRST_O, 0)
                    if is_unit(now, 3, 3):
                        gated_lo(0)
                        gated_lo(1)
                    if nxt:
                        maxima(*nxt, 0)
                        maxima(*nxt, 2)
                    if odd:
                        probs_out(*now, odd.pop(0))
                    if prev:
                        gate_unit(*prev)
                    if is_unit(now, 3, TOK):
                        gated_lo(2)
                        gated_lo(3)
                    if odd:
                        probs_out(*now, odd.pop(0))
                    if nxt:
                        normalise(*nxt)

                dve.wait_ge(kq_hi, L + 1)
                v.tensor_tensor(k_lo[:, 0:5 * P], kT[:, 0, 0:5 * P], k_hi[:, 0:5 * P].bitcast(f32),
                                ALU.subtract).then_inc(k_first, 1)
                v.tensor_tensor(q_lo[0][:, :], qT[:, 0, 0, :], q_hi[0][:, :].bitcast(f32), ALU.subtract).then_inc(k_first, 1)
                for h0 in (0, 2):
                    maxima(0, 0, h0)
                normalise(0, 0)
                m0, m1 = (4, 4) if L == 0 else (4, 2)
                n0, n1 = (2, 2) if L == 0 else (2, 1)
                per = TOK * (m0 + n0) + m1 + n1
                attention(dve, dve_step, chain, per)

                for p in range(1, PAIRS):
                    split_lo(L, FIRST_O, p)
                    for kt in (2 * p, 2 * p + 1):
                        if kt >= EARLY:
                            gated_lo(kt)
                dve.wait_ge(h_ready, H0[L] + 2 * KT)
                with dve.Fori(1, 4) as n:
                    chain.enter(n, 1, 1)
                    chunk(L, n + FIRST_O, "o", None)
                    chain.leave(4)
                gate_add(L, 3)
                for t in range(TT):
                    gate_out(L, 3, t)
                    if t > 0:
                        add_x(L, 3, t - 1)
                add_x(L, 3, TOK)

        @block.tensor
        def _(pe):
            mm = nc.tensor.matmul
            pe.sem_inc(o_done, CREDIT)
            pe.sem_inc(gated, CREDIT)
            pe.sem_inc(sc_done, 4 * CREDIT)
            pe.sem_inc(exp_done, 4)
            pe.sem_inc(xsq_l1, TT)
            pe.sem_inc(pt_act, 1)
            pe.sem_inc(pt_dve, 1)
            pe.wait_ge(const_made, 1)
            pe.wait_ge(s_rows, 80)
            nc.tensor.transpose(bank[7][:, 0:P], rows[:, :], ident[:, :]).then_inc(consts_T, 1)
            pe.wait_ge(cond_ready, 1)

            def mod_products(w, s, used):
                for kk in range(2):
                    k = 2 * s + kk
                    for j in range(4):
                        ins = mm(bank[MODBANK][32 * j:32 * j + 2, 0:256], cond[:, k, :], w[:, kk, j * 256:(j + 1) * 256],
                                 start=(k == 0), stop=(k == KT - 1))
                ins.then_inc(used, 1)

            def first_item(b, s):
                n = b * PAIRS + s
                if s == 0 and b > 0:
                    pe.wait_ge(mod_evac, b)
                pe.wait_ge(s_first[n % RING0], 32 * (n // RING0 + 1))
                mod_products(first_ring[n % RING0], s, first_used)

            def border_item(m):
                loads = len([n for n in range(GROUPS * PAIRS) if n % RING0 == m % BORDER0]) + m // BORDER0 + 1
                pe.wait_ge(s_first[m % BORDER0], 32 * loads)
                mod_products(first_ring[m % BORDER0], m, first_used)

            def mod_transpose(n, Q):
                pe.wait_ge(mod_evac, Q + 1)
                for h in range(2):
                    ins = nc.tensor.transpose(bank[7][:, h * P:(h + 1) * P], mod_ev[:, h * P:(h + 1) * P], ident[:, :])
                ins.then_inc(modT_done, 1)

            def chunk(L, ch, kind, X, mod=None, fresh=None, rows=None):
                C = ch + 14 * L
                start = isinstance(ch, int) and ch == 0 and L == 0
                for p in range(PAIRS):
                    for kk in range(2):
                        k = 2 * p + kk
                        if fresh == "x" and L == 0:
                            if k == 0:
                                pe.wait_ge(consts_ready, 1)
                                mod_transpose(0, 0)
                                h_transposes(L, 0)
                            if k % PER < PER - 1:
                                h_transposes(L, k + 1)
                        elif fresh == "x":
                            for kt in ((0, 1, 2) if k == 0 else (k + 2,)):
                                if kt < KT:
                                    h_transposes(L, kt)
                        if kk == 0:
                            pe.wait_ge(wlo_ready, C * PAIRS + (p + 1))
                        if fresh is not None:
                            pe.wait_ge(h_ready, H0[L] + (KT if fresh == "o" else 0) + k + 1)
                        for t in range(TT):
                            if k == 0 and not start:
                                pe.wait_ge(acc_free, C * TT + (t - 4))
                            hi, lo = hT_hi[:, k, t * P:(t + 1) * P], hT_lo[:, k, t * P:(t + 1) * P]
                            mm(bank[t][:, :], hi, w_hi[:, p % 2, kk], start=(k == 0), stop=False)
                            mm(bank[t][:, :], hi, w_lo[:, p % 2, kk], start=False, stop=False)
                            ins = mm(bank[t][:, :], lo, w_hi[:, p % 2, kk], start=False, stop=(k == KT - 1))
                            if fresh == "x" and L == 0 and k % PER == PER - 1 and k < KT - 1:
                                if t == 1:
                                    pe.wait_ge(h_ev, k + 1)
                                    mod_transpose(k // PER + 1, k // PER + 1)
                                elif t == 3:
                                    h_transposes(L, k + 1)
                            if k == KT - 1:
                                ins.then_inc(acc_done, 1)
                            elif kk == 1 and t == TT - 1:
                                ins.then_inc(mm_done, 1)
                        if fresh == "x" and L == 0 and k < KT - PER:
                            for i in range(3 * (k % PER), min(PAIRS, 3 * (k % PER) + 3)):
                                first_item(k // PER + 1, i)
                    if fresh == "x" and L == 1 and BORDER_ITEMS + p < PAIRS:
                        border_item(BORDER_ITEMS + p)
                    if mod is not None:
                        if p == 0:
                            pe.wait_ge(mod_evac, mod[1])
                        pe.wait_ge(s_mw[p % 2], mod[0] * 128 + 32 * (p // 2 + 1))
                        mod_products(mod_w[:, p % 2], p, mod_used)
                    if rows is not None and p == 0:
                        pe.wait_ge(tr_free, tr_number(L, X, 0))
                        mod_transpose(*rows)
                    if kind in ("k", "q", "z") and 1 <= p <= TT:
                        if rows is not None and p == 2:
                            pe.wait_ge(ab_ready, rows[0] + 1)
                        stage_transposes(L, kind, X, p - 1)
                    if kind == "v" and p == 2:
                        pe.wait_ge(s_ck, 16 * (L + 1))
                        pe.wait_ge(tr_free, N_TR * L + TT)
                        for h in range(4):
                            ins = nc.tensor.transpose(bank[7][:, h * P:(h + 1) * P], stage[:, 0, h * P:(h + 1) * P], ident[:, :])
                        ins.then_inc(tr_done, 1)

            def h_transposes(L, kt):
                if kt > 0:
                    pe.wait_ge(h_ev, H0[L] + kt)
                if L == 0 or kt == 0:
                    pe.wait_ge(ab_ready, kt // PER + 1 if L == 0 else 2 * GROUPS)
                for t in range(TT):
                    if kt % 4 == 0:
                        pe.wait_ge(x_normed, (4 * L + kt // 4) * TT + t + 1)
                    dst = bank[6][:, t * P:(t + 1) * P] if t < TOK else bank[7][:, 0:P]
                    ins = nc.tensor.transpose(dst, x_tok[:, t, kt * P:(kt + 1) * P], ident[:, :])
                ins.then_inc(h_tr, 1)

            def stage_transposes(L, kind, X, t):
                n = tr_number(L, X, t)
                if kind == "z":
                    pe.wait_ge(acc_free, (X - 5) * TT + (TT * (14 * L + FIRST_Z) + t + 1))
                else:
                    pe.wait_ge(roped, X * TT + (25 * L + t + 1))
                if isinstance(X, int) and X == 0 and t == 0:
                    pe.wait_ge(h_ev, H0[L] + KT)
                elif t == 0:
                    pe.wait_ge(tr_free, n)
                elif not (isinstance(n, int) and n == 1):
                    pe.wait_ge(tr_free, n - 1)
                for h in range(4):
                    ins = nc.tensor.transpose(bank[6 + t % 2][:, h * P:(h + 1) * P], stage[:, t, h * P:(h + 1) * P], ident[:, :])
                ins.then_inc(tr_done, 1)

            for s in range(PAIRS):
                first_item(0, s)
            for L in range(LAYERS):
                if L == 1:
                    for m in range(BORDER_ITEMS):
                        border_item(m)
                chunk(L, 0, None, None, fresh="x")
                chunk(L, 1, "k", 0, (0, 4) if L == 0 else (6, 11))
                chunk(L, 2, "v", None, (1, 5) if L == 0 else None)
                with pe.Fori(1, 4) as i:
                    chunk(L, i + 2, "q", i, (i + 1, i + 5) if L == 0 else None,
                          rows=(i + 3, i + 4) if L == 0 else None)
                chunk(L, FIRST_Z, "q", 4, (5, 9) if L == 0 else None, rows=(7, 8) if L == 0 else None)
                with pe.Fori(1, 4) as i:
                    chunk(L, i + FIRST_Z, "z", i + 4)

                def scores_ready(gg, u):
                    U = unit(L, gg, u)
                    if isinstance(gg, int) and gg == 0 and u == 0:
                        pe.wait_ge(k_first, 2 * (L + 1))
                    else:
                        pe.wait_ge(q_split, U - L)
                        if u == 0:
                            pe.wait_ge(kv_main, gg * 2 + 7 * L)
                    if u == TOK:
                        pe.wait_ge(kv_req, gg * 2 + (8 * L + 1))

                def scores(gg, u, heads):
                    U, b = unit(L, gg, u), buf(u)
                    def product(out, h, col, n, stop=True):
                        q = slice(h * P, (h + 1) * P)
                        mm(out, q_hi[b][:, q], k_hi[:, col:col + n], start=True, stop=False)
                        mm(out, q_hi[b][:, q], k_lo[:, col:col + n], start=False, stop=False)
                        return mm(out, q_lo[b][:, q], k_hi[:, col:col + n], start=False, stop=stop)

                    parts = key_parts(L, u)
                    masks = []
                    if L == 0 and 0 < u < TOK:
                        masks.append((0, mask_prev))
                    if L == 0 and u < TOK - 1:
                        masks.append((P if u == 0 else 2 * P, mask_next))
                    for h in heads:
                        pe.wait_ge(exp_done, U * 4 + (h + 1))
                        if len(parts) == 2:
                            product(bank[h][:, parts[0][1]:parts[0][1] + P], h, parts[1][0], P)
                        ins = product(bank[h][:, 0:parts[0][1]], h, *parts[0], stop=not masks)
                        for n, (at, mask) in enumerate(masks):
                            ins = mm(bank[h][:, at:at + P], ident_b[:, :], mask[:, :], start=False,
                                     stop=(n == len(masks) - 1))
                        ins.then_inc(sc_done, 1)
                    if L == 1 and u < TOK and 1 in heads:
                        pe.wait_ge(exp_done, U * 4 + 4)
                        for h in range(4):
                            ins = product(bank[4][:, h * P:(h + 1) * P], h, CTX, P)
                        ins.then_inc(scx_done, 1)

                def probs_T(gg, u, kt):
                    table, done = (n_even, pt_act) if kt % 2 == 0 else (n_odd, pt_dve)
                    if kt == 0:
                        pe.wait_ge(pn_ready, unit(L, gg, u) + 1)
                    pe.wait_ge(done, before(table, L, gg, u) + (kt // 2 + 1))
                    for h in range(4):
                        ins = nc.tensor.transpose(bank[5 + kt % 2][:, h * P:(h + 1) * P],
                                                  probs[buf(u)][:, h, kt * P:(kt + 1) * P], ident[:, :])
                    ins.then_inc(pt_done, 1)

                def value(gg, u, kt):
                    U, b, tiles = unit(L, gg, u), buf(u), key_tiles(L, u)
                    if kt == 0:
                        if u == 0:
                            pe.wait_ge(kv_main, gg * 2 + (7 * L + 1))
                        if u == TOK:
                            pe.wait_ge(kv_req, gg * 2 + (8 * L + 2))
                        pe.wait_ge(gated, U + CREDIT)
                    done, table = (pt_act, n_even) if kt % 2 == 0 else (pt_dve, n_odd)
                    pe.wait_ge(done, before(table, L, gg, u) + (kt // 2 + 2))
                    ins = mm(bank[7][:, :], v_g[:, tiles[kt], :], probsT[b][:, kt, :], start=(kt == 0),
                             stop=(kt == len(tiles) - 1))
                    if kt == len(tiles) - 1:
                        ins.then_inc(o_done, 1)

                def pe_step(prev, now, nxt):
                    v_tiles = list(range(n_kt[L][prev[1]])) if prev else []
                    p_tiles = list(range(n_kt[L][now[1]])) if now else []
                    if nxt:
                        scores_ready(*nxt)
                    for h in range(4):
                        if nxt:
                            scores(*nxt, [h])
                        if v_tiles and h > 0:
                            value(*prev, v_tiles.pop(0))
                        elif nxt and short(prev) and h == 2:
                            probs_T(*now, p_tiles.pop(0))
                    while v_tiles or p_tiles:
                        if p_tiles:
                            probs_T(*now, p_tiles.pop(0))
                        if v_tiles:
                            value(*prev, v_tiles.pop(0))

                scores_ready(0, 0)
                if L == 1:
                    pe.wait_ge(acc_free, TT * (14 * L + FIRST_O))
                for h in range(4):
                    if L == 0:
                        pe.wait_ge(acc_free, TT * (14 * L + FIRST_O - 1) + h + 1)
                    scores(0, 0, [h])
                for t in range(TT):
                    stage_transposes(L, "z", 8, t)
                pe.wait_ge(tr_free, N_TR * (L + 1))
                pe.wait_ge(mod_evac, 10 + 2 * L)
                attention(pe, pe_step)

                chunk(L, FIRST_O, None, None, fresh="o")
                with pe.Fori(1, 4) as n:
                    chunk(L, n + FIRST_O, None, None)


def rope_tables():
    n_tokens, grid_w, n_freq, theta = 512, 64, 32, 10000.0
    row, col = np.arange(n_tokens) // grid_w, np.arange(n_tokens) % grid_w
    inv = (np.float32(theta) ** (-np.arange(n_freq, dtype=np.float32) / n_freq)).astype(np.float32)
    ang = np.stack([row.astype(np.float32)[:, None] * inv, col.astype(np.float32)[:, None] * inv], axis=1)
    cos, sin = np.cos(ang).astype(np.float32), np.sin(ang).astype(np.float32)
    full_cos = np.stack([cos, cos], axis=2).reshape(n_tokens, 128)
    full_sin = np.stack([-sin, sin], axis=2).reshape(n_tokens, 128)
    return np.ascontiguousarray(full_cos), np.ascontiguousarray(full_sin)


_INS = ["x_prompt", "x_sample", "c", "cache_k", "cache_v", "c_ctx", "norm_g", "w_mod", "b_mod", "w_in",
        "q_norm_g", "k_norm_g", "sinks", "w_out"]
_OUTS = [("y_prompt", (1, 128, 2048)), ("y_sample", (1, 512, 2048)),
         ("new_cache_k", (1, 2, 128, 4, 128)), ("new_cache_v", (1, 2, 128, 4, 128))]


def kernel(**inputs):
    import concourse.bacc as bacc
    from concourse.bass_utils import run_bass_kernel_spmd

    nc = bacc.Bacc("TRN2", target_bir_lowering=False, num_devices=1)
    arrays = {f"in_{n}": np.ascontiguousarray(inputs[n]) for n in _INS}
    arrays["in_rope_cos"], arrays["in_rope_sin"] = rope_tables()
    args = [nc.dram_tensor(n, a.shape, mybir.dt.from_np(a.dtype), kind="ExternalInput").ap()
            for n, a in arrays.items()]
    args += [nc.dram_tensor(f"out_{n}", s, mybir.dt.float32, kind="ExternalOutput").ap() for n, s in _OUTS]
    build(nc, *args)
    r = run_bass_kernel_spmd(nc, [arrays], core_ids=[0])
    return tuple(r.results[0][f"out_{n}"] for n, _ in _OUTS)
```
